# Optimizing a Trainium2 kernel written in Bass

```python
import jax, jax.numpy as jnp
from jax import lax
import numpy as np

D_MODEL = 1024
BATCH = 1
SEQ = 512
DEPTH = 1

N_MIXERS = 3
HEAD_DIM = 64
N_HEADS = D_MODEL // HEAD_DIM
Q_DIM = N_HEADS * HEAD_DIM
Q_BLOCK = 128
ALIBI_MAX = 8.0
NORM_EPS = 1e-6
NEG_BIG = -1e30
FORCE_SCORE = 1e4

NSA_KV_HEADS = 4
NSA_GROUP = N_HEADS // NSA_KV_HEADS
NSA_KV_DIM = NSA_KV_HEADS * HEAD_DIM
CMP_BLOCK = 32
CMP_STRIDE = 16
CMP_HIDDEN = 256
SEL_BLOCK = 64
N_SELECT = 16
NSA_WINDOW = 512
NSA_IN = Q_DIM + 6 * NSA_KV_DIM + 3 * N_HEADS

SWA_KV_HEADS = 2
SWA_GROUP = N_HEADS // SWA_KV_HEADS
SWA_KV_DIM = SWA_KV_HEADS * HEAD_DIM
SWA_WINDOW = 128
SWA_IN = Q_DIM + 2 * SWA_KV_DIM

FOX_HEADS = N_HEADS
FOX_IN = 3 * Q_DIM + FOX_HEADS

D_FF = 2816
CONV_WIDTH = 3

N_NSA_LAYERS = (DEPTH - 0 + N_MIXERS - 1) // N_MIXERS
N_SWA_LAYERS = (DEPTH - 1 + N_MIXERS - 1) // N_MIXERS
N_FOX_LAYERS = (DEPTH - 2 + N_MIXERS - 1) // N_MIXERS

kernel_name = 'hybrid_nsa_swa_fox_convglu'

def rmsnorm(x, g):
    xf = x.astype(jnp.float32)
    y = xf * lax.rsqrt(jnp.mean(xf * xf, axis=-1, keepdims=True) + NORM_EPS)
    return (y * g.astype(jnp.float32)).astype(x.dtype)

def alibi_slopes(n_heads):
    return jnp.asarray(2.0 ** (-ALIBI_MAX * np.arange(1, n_heads + 1) / n_heads), dtype=jnp.float32)

def masked_softmax(s, mask):
    p = jax.nn.softmax(jnp.where(mask, s, NEG_BIG), axis=-1)
    return jnp.where(mask, p, 0.0)

def nsa_mixer(h, w_in, cmp_pos, cmp_w1, cmp_w2, w_out):
    B, T, _ = h.shape
    G, R, Dh = NSA_KV_HEADS, NSA_GROUP, HEAD_DIM
    f32 = jnp.float32
    scale = Dh ** -0.5
    splits = [Q_DIM + i * NSA_KV_DIM for i in range(7)]
    q, kc, vc, ks, vs, kw, vw, gate_logit = jnp.split(h @ w_in, splits, axis=-1)
    q = q.reshape(B, T, G, R, Dh)
    kc, vc, ks, vs, kw, vw = [a.reshape(B, T, G, Dh) for a in (kc, vc, ks, vs, kw, vw)]
    gates = jax.nn.sigmoid(gate_logit.astype(f32)).reshape(B, T, G, R, 3)
    slopes = alibi_slopes(N_HEADS).reshape(G, R)

    n_cmp = (T - CMP_BLOCK) // CMP_STRIDE + 1
    cmp_start = np.arange(n_cmp) * CMP_STRIDE
    cmp_idx = cmp_start[:, None] + np.arange(CMP_BLOCK)[None, :]

    def compress(a, pos, w1, w2):
        blk = a[:, cmp_idx] + pos[None, None, :, None, :].astype(a.dtype)
        blk = blk.transpose(0, 1, 3, 2, 4).reshape(B, n_cmp, G, CMP_BLOCK * Dh)
        return jax.nn.gelu(blk @ w1) @ w2

    k_cmp = compress(kc, cmp_pos[0], cmp_w1[0], cmp_w2[0])
    v_cmp = compress(vc, cmp_pos[1], cmp_w1[1], cmp_w2[1]).astype(f32)
    cmp_end = jnp.asarray(cmp_start + CMP_BLOCK - 1, dtype=jnp.int32)

    n_sel = T // SEL_BLOCK
    sel_start = np.arange(n_sel) * SEL_BLOCK
    overlap = np.clip(np.minimum(cmp_start[:, None] + CMP_BLOCK, sel_start[None, :] + SEL_BLOCK)
                      - np.maximum(cmp_start[:, None], sel_start[None, :]), 0, None) / CMP_BLOCK
    overlap = jnp.asarray(overlap, dtype=f32)
    k_top = min(N_SELECT, n_sel)
    ks_blk = ks.reshape(B, n_sel, SEL_BLOCK, G, Dh).transpose(0, 3, 1, 2, 4)
    vs_blk = vs.reshape(B, n_sel, SEL_BLOCK, G, Dh).transpose(0, 3, 1, 2, 4)
    b_idx = jnp.arange(B)[:, None, None, None]
    g_idx = jnp.arange(G)[None, :, None, None]
    blk_ids = jnp.arange(n_sel, dtype=jnp.int32)

    kw_pad = jnp.pad(kw, ((0, 0), (NSA_WINDOW, 0), (0, 0), (0, 0)))
    vw_pad = jnp.pad(vw, ((0, 0), (NSA_WINDOW, 0), (0, 0), (0, 0)))
    win_off = jnp.arange(Q_BLOCK + NSA_WINDOW, dtype=jnp.int32) - NSA_WINDOW

    def query_block(c):
        t0 = c * Q_BLOCK
        tq = t0 + jnp.arange(Q_BLOCK, dtype=jnp.int32)
        qc = lax.dynamic_slice_in_dim(q, t0, Q_BLOCK, axis=1)
        gc = lax.dynamic_slice_in_dim(gates, t0, Q_BLOCK, axis=1)

        d_cmp = tq[:, None] - cmp_end[None, :]
        s = jnp.einsum('bqgrd,bngd->bgrqn', qc, k_cmp).astype(f32) * scale
        s = s - slopes[None, :, :, None, None] * d_cmp.astype(f32)
        p_cmp = masked_softmax(s, d_cmp >= 0)
        o_cmp = jnp.einsum('bgrqn,bngd->bqgrd', p_cmp, v_cmp)

        imp = jnp.einsum('bgrqn,nj->bgqj', p_cmp, overlap)
        cur = (tq // SEL_BLOCK)[:, None]
        forced = (blk_ids[None, :] == 0) | (blk_ids[None, :] == cur) | (blk_ids[None, :] == cur - 1)
        imp = jnp.where(forced, FORCE_SCORE, jnp.where(blk_ids[None, :] <= cur, imp, -1.0))
        _, sel = lax.top_k(imp, k_top)
        k_sel = ks_blk[b_idx, g_idx, sel].reshape(B, G, Q_BLOCK, k_top * SEL_BLOCK, Dh)
        v_sel = vs_blk[b_idx, g_idx, sel].reshape(B, G, Q_BLOCK, k_top * SEL_BLOCK, Dh).astype(f32)
        pos = (sel[..., None] * SEL_BLOCK + jnp.arange(SEL_BLOCK, dtype=jnp.int32)).reshape(B, G, Q_BLOCK, k_top * SEL_BLOCK)
        d_sel = (tq[None, None, :, None] - pos)[:, :, None]
        s = jnp.einsum('bqgrd,bgqxd->bgrqx', qc, k_sel).astype(f32) * scale
        s = s - slopes[None, :, :, None, None] * d_sel.astype(f32)
        p_sel = masked_softmax(s, d_sel >= 0)
        o_sel = jnp.einsum('bgrqx,bgqxd->bqgrd', p_sel, v_sel)

        kwc = lax.dynamic_slice_in_dim(kw_pad, t0, Q_BLOCK + NSA_WINDOW, axis=1)
        vwc = lax.dynamic_slice_in_dim(vw_pad, t0, Q_BLOCK + NSA_WINDOW, axis=1).astype(f32)
        sk = t0 + win_off
        d_win = tq[:, None] - sk[None, :]
        win_mask = (d_win >= 0) & (d_win < NSA_WINDOW) & (sk[None, :] >= 0)
        s = jnp.einsum('bqgrd,bkgd->bgrqk', qc, kwc).astype(f32) * scale
        s = s - slopes[None, :, :, None, None] * d_win.astype(f32)
        p_win = masked_softmax(s, win_mask)
        o_win = jnp.einsum('bgrqk,bkgd->bqgrd', p_win, vwc)

        o = gc[..., 0:1] * o_cmp + gc[..., 1:2] * o_sel + gc[..., 2:3] * o_win
        return o.astype(h.dtype)

    o = lax.map(query_block, jnp.arange(T // Q_BLOCK))
    o = jnp.moveaxis(o, 0, 1).reshape(B, T, Q_DIM)
    return o @ w_out

def swa_sink_mixer(h, w_in, sinks, w_out):
    B, T, _ = h.shape
    G, R, Dh = SWA_KV_HEADS, SWA_GROUP, HEAD_DIM
    f32 = jnp.float32
    nb = T // Q_BLOCK
    q, k, v = jnp.split(h @ w_in, [Q_DIM, Q_DIM + SWA_KV_DIM], axis=-1)
    q = q.reshape(B, nb, Q_BLOCK, G, R, Dh)
    k = k.reshape(B, nb, Q_BLOCK, G, Dh)
    v = v.reshape(B, nb, Q_BLOCK, G, Dh)

    def with_previous_block(a):
        prev = jnp.pad(a[:, :-1], ((0, 0), (1, 0), (0, 0), (0, 0), (0, 0)))
        return jnp.concatenate([prev, a], axis=2)

    kk, vv = with_previous_block(k), with_previous_block(v).astype(f32)
    rel_q = jnp.arange(Q_BLOCK, dtype=jnp.int32)
    rel_k = jnp.arange(2 * Q_BLOCK, dtype=jnp.int32) - Q_BLOCK
    dist = rel_q[:, None] - rel_k[None, :]
    abs_k = (jnp.arange(nb, dtype=jnp.int32) * Q_BLOCK)[:, None] + rel_k[None, :]
    mask = ((dist >= 0) & (dist < SWA_WINDOW))[None] & (abs_k >= 0)[:, None, :]
    slopes = alibi_slopes(N_HEADS).reshape(G, R)
    s = jnp.einsum('bnqgrd,bnkgd->bngrqk', q, kk).astype(f32) * Dh ** -0.5
    s = s - slopes[:, :, None, None] * dist.astype(f32)
    s = jnp.where(mask[None, :, None, None], s, NEG_BIG)
    sink = jnp.broadcast_to(sinks.astype(f32).reshape(G, R)[:, :, None, None], s.shape[:-1] + (1,))
    p = jax.nn.softmax(jnp.concatenate([s, sink], axis=-1), axis=-1)[..., :-1]
    o = jnp.einsum('bngrqk,bnkgd->bnqgrd', p, vv)
    return o.reshape(B, T, Q_DIM).astype(h.dtype) @ w_out

def fox_mixer(h, w_in, f_bias, w_out):
    B, T, _ = h.shape
    H, Dh = FOX_HEADS, HEAD_DIM
    f32 = jnp.float32
    q, k, v, f_logit = jnp.split(h @ w_in, [Q_DIM, 2 * Q_DIM, 3 * Q_DIM], axis=-1)
    q = q.reshape(B, T, H, Dh)
    k = k.reshape(B, T, H, Dh)
    v = v.reshape(B, T, H, Dh).astype(f32)
    log_f = jax.nn.log_sigmoid(f_logit.astype(f32) + f_bias.astype(f32))
    cum = jnp.cumsum(log_f, axis=1).transpose(0, 2, 1)
    t_k = jnp.arange(T, dtype=jnp.int32)

    def query_block(c):
        t0 = c * Q_BLOCK
        tq = t0 + jnp.arange(Q_BLOCK, dtype=jnp.int32)
        qc = lax.dynamic_slice_in_dim(q, t0, Q_BLOCK, axis=1)
        cq = lax.dynamic_slice_in_dim(cum, t0, Q_BLOCK, axis=2)
        s = jnp.einsum('bqhd,bkhd->bhqk', qc, k).astype(f32) * Dh ** -0.5
        s = s + cq[..., :, None] - cum[..., None, :]
        p = masked_softmax(s, t_k[None, :] <= tq[:, None])
        return jnp.einsum('bhqk,bkhd->bqhd', p, v).astype(h.dtype)

    o = lax.map(query_block, jnp.arange(T // Q_BLOCK))
    o = jnp.moveaxis(o, 0, 1).reshape(B, T, Q_DIM)
    return o @ w_out

def conv_glu_mlp(h, w_up, conv_w, conv_b, w_down):
    T = h.shape[1]
    u = h @ w_up
    u_pad = jnp.pad(u, ((0, 0), (CONV_WIDTH - 1, 0), (0, 0)))
    w = conv_w.astype(u.dtype)
    u = sum(w[i] * u_pad[:, i:i + T] for i in range(CONV_WIDTH)) + conv_b.astype(u.dtype)
    a, g = jnp.split(u, 2, axis=-1)
    return (jax.nn.silu(g) * a) @ w_down

def setup_inputs(seed: int = 0) -> dict:
    key = jax.random.key(seed)
    k = jax.random.split(key, 20)

    def dense(kk, shape, fan_in):
        return jax.random.normal(kk, shape, jnp.float32) * fan_in ** -0.5

    def gain(kk, shape):
        return 1.0 + 0.05 * jax.random.normal(kk, shape, jnp.float32)

    return {
        'x': jax.random.normal(k[0], (BATCH, SEQ, D_MODEL), jnp.float32),
        'attn_norm': gain(k[1], (DEPTH, D_MODEL)),
        'mlp_norm': gain(k[2], (DEPTH, D_MODEL)),
        'final_norm': gain(k[3], (D_MODEL,)),
        'nsa_w_in': dense(k[4], (N_NSA_LAYERS, D_MODEL, NSA_IN), D_MODEL),
        'nsa_cmp_pos': 0.1 * jax.random.normal(k[5], (N_NSA_LAYERS, 2, CMP_BLOCK, HEAD_DIM), jnp.float32),
        'nsa_cmp_w1': dense(k[6], (N_NSA_LAYERS, 2, CMP_BLOCK * HEAD_DIM, CMP_HIDDEN), CMP_BLOCK * HEAD_DIM),
        'nsa_cmp_w2': dense(k[7], (N_NSA_LAYERS, 2, CMP_HIDDEN, HEAD_DIM), CMP_HIDDEN),
        'nsa_w_out': dense(k[8], (N_NSA_LAYERS, Q_DIM, D_MODEL), Q_DIM),
        'swa_w_in': dense(k[9], (N_SWA_LAYERS, D_MODEL, SWA_IN), D_MODEL),
        'swa_sinks': 0.5 * jax.random.normal(k[10], (N_SWA_LAYERS, N_HEADS), jnp.float32),
        'swa_w_out': dense(k[11], (N_SWA_LAYERS, Q_DIM, D_MODEL), Q_DIM),
        'fox_w_in': dense(k[12], (N_FOX_LAYERS, D_MODEL, FOX_IN), D_MODEL),
        'fox_f_bias': jax.random.uniform(k[13], (N_FOX_LAYERS, FOX_HEADS), jnp.float32, minval=2.0, maxval=5.0),
        'fox_w_out': dense(k[14], (N_FOX_LAYERS, Q_DIM, D_MODEL), Q_DIM),
        'mlp_w_up': dense(k[15], (DEPTH, D_MODEL, 2 * D_FF), D_MODEL),
        'mlp_conv_w': dense(k[16], (DEPTH, CONV_WIDTH, 2 * D_FF), CONV_WIDTH),
        'mlp_conv_b': 0.02 * jax.random.normal(k[17], (DEPTH, 2 * D_FF), jnp.float32),
        'mlp_w_down': dense(k[18], (DEPTH, D_FF, D_MODEL), D_FF),
    }

def reference(x, attn_norm, mlp_norm, final_norm, nsa_w_in, nsa_cmp_pos, nsa_cmp_w1, nsa_cmp_w2, nsa_w_out,
              swa_w_in, swa_sinks, swa_w_out, fox_w_in, fox_f_bias, fox_w_out,
              mlp_w_up, mlp_conv_w, mlp_conv_b, mlp_w_down):
    for i in range(DEPTH):
        kind, j = i % N_MIXERS, i // N_MIXERS
        h = rmsnorm(x, attn_norm[i])
        if kind == 0:
            y = nsa_mixer(h, nsa_w_in[j], nsa_cmp_pos[j], nsa_cmp_w1[j], nsa_cmp_w2[j], nsa_w_out[j])
        elif kind == 1:
            y = swa_sink_mixer(h, swa_w_in[j], swa_sinks[j], swa_w_out[j])
        else:
            y = fox_mixer(h, fox_w_in[j], fox_f_bias[j], fox_w_out[j])
        x = x + y
        x = x + conv_glu_mlp(rmsnorm(x, mlp_norm[i]), mlp_w_up[i], mlp_conv_w[i], mlp_conv_b[i], mlp_w_down[i])
    return rmsnorm(x, final_norm)


_drawn_inputs = setup_inputs


def setup_inputs(seed=0):
    import zlib

    import numpy as np

    out = dict(_drawn_inputs(seed))
    spreads = {}
    factors = {'mlp_conv_b': 4.121}
    for name, (base, spread) in spreads.items():
        noise = np.random.default_rng([zlib.crc32(name.encode()), seed]).standard_normal(out[name].shape)
        drawn = base * np.exp(spread * noise) if base else spread * noise
        out[name] = __import__('jax').numpy.asarray(drawn.astype(out[name].dtype))
    for name, factor in factors.items():
        out[name] = (out[name] * factor).astype(out[name].dtype)
    return out
```

```python
from contextlib import ExitStack

import concourse.bass as bass
from concourse import mybir

F32 = mybir.dt.float32
F32R = mybir.dt.float32r
ALU = mybir.AluOpType
ACT = mybir.ActivationFunctionType
AX = mybir.AxisListType.X

P = 128
T = 512
D = 1024
TB = T // P
KT = D // P
HD = 64
HEADS = D // HD
GROUPS = 4
R = HEADS // GROUPS
KV = GROUPS * HD
COL_KC, COL_VC, COL_KS, COL_VS, COL_KW, COL_VW, COL_GATE = (D + n * KV for n in range(7))
W_IN = COL_GATE + 3 * HEADS
COL_GATE_TILE = W_IN - P
GATE_ROW = P - 3 * HEADS
CMP, STRIDE = 32, 16
NC = T // STRIDE
TP = T + CMP // 2
CJ = CMP * HD // P
HID = 256
FF = 2816
FT = FF // P
EPS = 1e-6
SCALE = HD ** -0.5
MASKED = 1e32
GELU_C = 0.7978845608028654
SLOPE_STEP = 2.0 ** (-8.0 * R / HEADS)

RING = 4
N_GATE = 0
N_CMP = 1
N_GRP = N_CMP + GROUPS
N_OUT = N_GRP + 4 * GROUPS
N_UP = N_OUT + KT
N_DOWN = N_UP + 2 * FT
N_END = N_DOWN + FT
UNITS = 2 * TB
PT_UNITS = 1 + 2 * TB
V_ANORM, V_MNORM, V_POS, V_CB = 0, KT, 2 * KT, 2 * KT + 2 * CJ
V_A = V_CB + 2 * FT
V_CW = V_A
N_CONST = 11


def slot(n):
    return (n + 3) % RING


def slopes():
    return [2.0 ** (-8.0 * (r + 1) / HEADS) for r in range(R)]


def poff(i):
    return P * i * (i + 1) // 2


def build(nc, x, attn_norm, mlp_norm, final_norm, nsa_w_in, cmp_pos, cmp_w1, cmp_w2, nsa_w_out, mlp_w_up, conv_w, conv_b, mlp_w_down, out):
    ctx = ExitStack()
    w_in, w_out, w_up, w_down = (w[0] for w in (nsa_w_in, nsa_w_out, mlp_w_up, mlp_w_down))
    with ctx:
        place = {"at": (nc.sbuf_base + 31) // 32 * 32}

        def sb(name, shape, dt=F32, at=None):
            size = 4
            for s in shape[1:]:
                size *= s
            off = place["at"] if at is None else at
            if at is None:
                place["at"] = off + (size + 31) // 32 * 32
            assert off + size <= nc.sbuf_usable_end, (name, off + size)
            return nc.alloc_sbuf_tensor_at(name, shape, dt, offset=off), off + (size + 31) // 32 * 32

        def keep(name, shape, dt=F32):
            return sb(name, shape, dt)[0]

        def sem(name):
            return ctx.enter_context(nc.semaphore(name))

        ident = keep("ident", [P, P])
        vec = keep("vec", [P, V_CW + 3 * 2 * FT])
        half_pow = keep("half_pow", [P, TB])
        sumsq = keep("sumsq", [P, 3, TB])
        meansq = keep("meansq", [P, 3, TB])
        rstd = keep("rstd", [P, 3, TB])
        gates = keep("gates", [P, HEADS, 3, TB])
        valid = keep("valid", [P, 1])
        bias = keep("bias", [P, R, T])
        bias_c = keep("bias_c", [P, R, TB, NC])
        kkc_h = keep("kkc_h", [P, GROUPS, NC], F32R)
        kkc_l = keep("kkc_l", [P, GROUPS, NC], F32R)
        vvc_all = keep("vvc_all", [P, GROUPS, HD])
        xs = keep("xs", [P, TB, D])
        hT_h = keep("hT_h", [P, KT, T], F32R)
        hT_l = keep("hT_l", [P, KT, T], F32R)
        raw = keep("raw", [P, RING, D])
        wh = keep("wh", [P, RING, D], F32R)
        wl = keep("wl", [P, RING, D], F32R)
        base = place["at"]

        def region(specs, at=base):
            made = []
            for name, shape, dt in specs:
                t, at = sb(name, shape, dt, at=at)
                made.append(t)
            return made

        stage, xn, = region([("stage", [P, 3, P], F32), ("xn", [P, TB, D], F32)])
        w1raw, w1h, w1l, kc2, vc2, blk_h, blk_l, gel, gel2, gT, gTr, w2d, w2v, glT = region([
            ("w1raw", [P, CJ, HID], F32), ("w1h", [P, CJ, HID], F32R), ("w1l", [P, CJ, HID], F32R),
            ("kc2", [P, GROUPS, TP], F32), ("vc2", [P, GROUPS, TP], F32),
            ("blk_h", [P, CJ, GROUPS, NC], F32R), ("blk_l", [P, CJ, GROUPS, NC], F32R),
            ("gel", [P, HID], F32), ("gel2", [P, HID], F32), ("gT", [P, 2, GROUPS * NC], F32),
            ("gTr", [P, GROUPS, 2, TB, NC], F32), ("w2d", [P, 2, 2, HD], F32), ("w2v", [P, 2, HD], F32),
            ("glT", [P, T], F32)], at=base + 3 * P * 4 + TB * D * 4)
        (qq, kk_h, kk_l, vv, vvc, prob, sc_c, pbd, pt_h, pt_l, mn, mn_c, sums, rs, vT, otmp, osum, oT_h, oT_l) = region([
            ("qq", [P, R, T], F32R), ("kk_h", [P, 2, T], F32R), ("kk_l", [P, 2, T], F32R),
            ("vv", [P, 2, TB, 2, HD], F32R), ("vvc", [P, 2, HD], F32R),
            ("prob", [P, 2, 2, poff(TB)], F32), ("sc_c", [P, 2, TB, NC], F32), ("pbd", [P, 2, TB, TB, NC], F32),
            ("pt_h", [P, 2, T], F32R), ("pt_l", [P, 2, T], F32R),
            ("mn", [P, 2, UNITS], F32), ("mn_c", [P, 2, TB], F32), ("sums", [P, 2, 3, TB], F32), ("rs", [P, 2, 3, TB], F32),
            ("vT", [P, T], F32), ("otmp", [P, T], F32), ("osum", [P, 2, T], F32),
            ("oT_h", [P, KT, T], F32R), ("oT_l", [P, KT, T], F32R)])
        aT_h, aT_l, conv, th, act, fgain = region([
            ("aT_h", [P, FT, T], F32R), ("aT_l", [P, FT, T], F32R),
            ("conv", [P, RING, T], F32), ("th", [P, 2, T], F32), ("act", [P, 2, T], F32), ("fgain", [P, D], F32)],
            at=base)
        x1n, = region([("x1n", [P, TB, D], F32)], at=base)
        yT, = region([("yT", [P, KT, T], F32)], at=base)

        bank = [ctx.enter_context(nc.psum_tensor(f"bank{n}", [P, 512], F32)) for n in range(8)]
        pj = bank[0:2]
        sc = bank[2:4]
        tr = bank[4:6]
        cc, ob = bank[6], bank[7]

        x_in = [sem(f"x_in{t}") for t in range(TB)]
        vec_in = sem("vec_in")
        w1_in = [sem(f"w1_in{c}") for c in range(2)]
        w2_in = sem("w2_in")
        raw_in = [sem(f"raw_in{s}") for s in range(RING)]
        fgain_in = sem("fgain_in")
        stored = sem("stored")
        const_ready = sem("const_ready")
        stage_clear = sem("stage_clear")
        wh_done, wl_done, tile_done = sem("wh_done"), sem("wl_done"), sem("tile_done")
        sq_done, rstd_done, xn_done = sem("sq_done"), sem("rstd_done"), sem("xn_done")
        vecT_ready, vec_done = sem("vecT_ready"), sem("vec_done")
        xT_ready, hT_h_done, hT_done = sem("xT_ready"), sem("hT_h_done"), sem("hT_done")
        pj_evac = sem("pj_evac")
        glT_done, gateT_ready, gate_tanh, gates_done = sem("glT_done"), sem("gateT_ready"), sem("gate_tanh"), sem("gates_done")
        c_copied = sem("c_copied")
        w1h_done, w1l_done, blkh_done, blk_done = sem("w1h_done"), sem("w1l_done"), sem("blkh_done"), sem("blk_done")
        hid_ready, gel_step, gel_tanh, gelT_ready, gT_done = sem("hid_ready"), sem("gel_step"), sem("gel_tanh"), sem("gelT_ready"), sem("gT_done")
        cmp_ready, kkch_done, cmp_done = sem("cmp_ready"), sem("kkch_done"), sem("cmp_done")
        bias_done = sem("bias_done")
        kvh_done, vT_done, gel_mid = sem("kvh_done"), sem("vT_done"), sem("gel_mid")
        vvc_done = sem("vvc_done")
        qh_done = sem("qh_done")
        scores_ready, masked, exp_done = sem("scores_ready"), sem("masked"), sem("exp_done")
        cc_ready, cc_biased, c_min, c_shifted, c_exp = sem("cc_ready"), sem("cc_biased"), sem("c_min"), sem("c_shifted"), sem("c_exp")
        c_sum, recip_done, rs_done, p_ready = sem("c_sum"), sem("recip_done"), sem("rs_done"), sem("p_ready")
        tr_ready, pth_done, pt_done, av_done = sem("tr_ready"), sem("pth_done"), sem("pt_done"), sem("av_done")
        o_copied, o_summed, oh_done, oT_done = sem("o_copied"), sem("o_summed"), sem("oh_done"), sem("oT_done")
        mask_begun = sem("mask_begun")
        y_ready, x1_done = sem("y_ready"), sem("x1_done")
        conv0, conv1, conv_done = sem("conv0"), sem("conv1"), sem("conv_done")
        g_tanh, silu_done, act_done, ah_done, aT_done = sem("g_tanh"), sem("silu_done"), sem("act_done"), sem("ah_done"), sem("aT_done")
        yT_ready, yT_act, yT_dve, z_ready, x2_done = sem("yT_ready"), sem("yT_act"), sem("yT_dve"), sem("z_ready"), sem("x2_done")
        out_done = sem("out_done")
        C_MASKED = 2
        C_CC = 1
        C_TR = 2 * PT_UNITS
        C_PT = 2
        C_AV = 2
        C_O = 1
        C_CONV = RING
        C_AH = 2

        block = ctx.enter_context(nc.Block())

        def stream_wait(eng, n, m4=None):
            s, k = slot(n), (n + 3) // RING + (slot(n) == 3)
            eng.wait_ge(raw_in[s], 32 * k if m4 is None else 32 * (m4 + k))

        @block.sync
        def _(sp):
            def tile_dma(n, halves, more=None):
                s = slot(n)
                if n >= RING:
                    sp.wait_ge(wl_done, n - RING + 1 if more is None else n - RING + 1 + RING * more)
                for dst, src in halves:
                    sp.dma_start(dst, src).then_inc(raw_in[s], 16)

            def cols(w, s, c0, width=P, at=0):
                src = w.rearrange("(k p) c -> p k c", p=P)
                dst = raw[:, s, :].rearrange("p (k c) -> p k c", c=P)
                return [(dst[:, 4 * h:4 * h + 4, at:at + width], src[:, 4 * h:4 * h + 4, bass.ds(c0, width)]) for h in range(2)]

            def pair(w, s, c0, c1):
                src = w.rearrange("(k p) c -> p k c", p=P)
                dst = raw[:, s, :].rearrange("p (k c) -> p k c", c=P)
                return [(dst[:, :, HD * h:HD * h + HD], src[:, :, bass.ds(c, HD)]) for h, c in enumerate((c0, c1))]

            def rows(w, s, r0):
                return [(raw[:, s, 512 * h:512 * h + 512], w[bass.ds(r0, P), 512 * h:512 * h + 512]) for h in range(2)]

            for t in range(TB):
                sp.dma_start(xs[:, t, :], x[0, t * P:(t + 1) * P, :]).then_inc(x_in[t], 16)
            tile_dma(N_GATE, cols(w_in, slot(N_GATE), COL_GATE_TILE))
            for g in range(GROUPS):
                tile_dma(N_CMP + g, pair(w_in, slot(N_CMP + g), COL_KC + HD * g, COL_VC + HD * g))

            def group(g, more=None):
                tile_dma(N_GRP, pair(w_in, slot(N_GRP), COL_KS + g * HD, COL_KW + g * HD), g)
                tile_dma(N_GRP + 1, pair(w_in, slot(N_GRP + 1), COL_VS + g * HD, COL_VW + g * HD), g)
                for q in range(2):
                    tile_dma(N_GRP + 2 + q, cols(w_in, slot(N_GRP + 2 + q), g * R * HD + q * P), g)

            with sp.Fori(0, GROUPS) as g:
                group(g)
            with sp.Fori(0, KT // RING) as i:
                for j in range(RING):
                    tile_dma(N_OUT + j, rows(w_out, slot(N_OUT + j), i * (RING * P) + j * P), i)
            with sp.Fori(0, FT // 2) as i:
                for j in range(RING):
                    tile_dma(N_UP + j, cols(w_up, slot(N_UP + j), i * (2 * P) + (j // 2) * P + (j % 2) * FF), i)
            for k in range(2):
                tile_dma(N_DOWN + k, rows(w_down, slot(N_DOWN + k), k * P))
            with sp.Fori(0, (FT - 2) // RING) as i:
                for j in range(RING):
                    tile_dma(N_DOWN + 2 + j, rows(w_down, slot(N_DOWN + 2 + j), i * (RING * P) + (2 + j) * P), i)
            for t in range(TB):
                sp.wait_ge(out_done, t + 1)
                sp.dma_start(out[0, t * P:(t + 1) * P, :], xs[:, t, :]).then_inc(stored, 16)
            sp.wait_ge(stored, 16 * TB)

        @block.gpsimd
        def _(pool):
            g = nc.gpsimd
            step = [0]

            def then(ins, wait=True):
                step[0] += 1
                ins.then_inc(const_ready, 1)
                if wait:
                    pool.wait_ge(const_ready, step[0])

            g.memset(stage[:, :, :], 0.0).then_inc(stage_clear, 1)
            then(g.memset(half_pow[:, :], -0.5), False)
            then(g.memset(ident[:, :], 0.0))
            then(g.affine_select(out=ident[:, :], in_=ident[:, :], compare_op=ALU.not_equal, fill=1.0, base=0,
                                 pattern=[[-1, P]], channel_multiplier=1))
            then(g.memset(valid[:, :], 1.0))
            then(g.affine_select(out=valid[:, :], in_=valid[:, :], compare_op=ALU.is_ge, fill=0.0, base=-(CMP - 1),
                                 pattern=[[0, 1]], channel_multiplier=1))
            dist, dist_c = bias[:, R - 1, :], bias_c[:, R - 1, :, :]
            then(g.iota(dist, pattern=[[-1, T]], base=T - P, channel_multiplier=1, allow_small_or_imprecise_dtypes=True))
            then(g.affine_select(out=dist, in_=dist, compare_op=ALU.is_ge, fill=MASKED, base=T - P,
                                 pattern=[[-1, T]], channel_multiplier=1))
            then(g.iota(dist_c, pattern=[[P, TB], [-STRIDE, NC]], base=-(CMP - 1), channel_multiplier=1,
                        allow_small_or_imprecise_dtypes=True))
            then(g.affine_select(out=dist_c, in_=dist_c, compare_op=ALU.is_ge, fill=MASKED, base=-(CMP - 1),
                                 pattern=[[P, TB], [-STRIDE, NC]], channel_multiplier=1))

            for z in (kc2, vc2):
                then(g.memset(z[:, :, T - 1:TP], 0.0))
            assert step[0] == N_CONST

            def rms(which):
                for t in range(TB):
                    pool.wait_ge(sq_done, TB * which + t + 1)
                    g.tensor_scalar(meansq[:, which, t:t + 1], sumsq[:, which, t:t + 1], 1.0 / D, EPS, ALU.mult, ALU.add)\
                        .then_inc(const_ready, 1)
                    step[0] += 1
                    pool.wait_ge(const_ready, step[0])
                    g.tensor_tensor(rstd[:, which, t:t + 1], meansq[:, which, t:t + 1], half_pow[:, t:t + 1], ALU.pow)\
                        .then_inc(rstd_done, 1)

            def low(n, more=None):
                s = slot(n)
                pool.wait_ge(wh_done, n + 1 if more is None else n + 1 + RING * more)
                g.tensor_tensor(wl[:, s, :], raw[:, s, :], wh[:, s, :].bitcast(F32), ALU.subtract).then_inc(wl_done, 1)

            low(N_GATE)
            rms(0)
            with pool.Fori(0, (N_OUT + RING - N_CMP) // RING) as i:
                for j in range(RING):
                    low(N_CMP + j, i)
            for n in range(N_OUT + RING, N_UP + RING):
                low(n)
            rms(1)
            with pool.Fori(0, (N_DOWN + FT - 2 - N_UP - RING) // RING) as i:
                for j in range(RING):
                    low(N_UP + RING + j, i)
            for n in range(N_END - 2, N_END):
                low(n)
            rms(2)

        @block.scalar
        def _(act_):
            a = nc.scalar

            def high(n, more=None):
                s = slot(n)
                stream_wait(act_, n, more)
                if n >= RING:
                    act_.wait_ge(tile_done, n - RING + 1 if more is None else n - RING + 1 + RING * more)
                a.activation(wh[:, s, :], raw[:, s, :], ACT.Copy).then_inc(wh_done, 1)

            act_.wait_ge(stage_clear, 1)
            row = 0
            for src, n in ((attn_norm.rearrange("a (k p) -> (a k) p", p=P), KT), (mlp_norm.rearrange("a (k p) -> (a k) p", p=P), KT),
                           (cmp_pos[0].rearrange("c (j a) d -> (c j) (a d)", a=2), 2 * CJ),
                           (conv_b.rearrange("a (m p) -> (a m) p", p=P), 2 * FT)):
                a.dma_start(stage[row:row + n, 0, :], src).then_inc(vec_in, 16)
                row += n
            taps = conv_w[0].rearrange("i (m p) -> (i m) p", p=P)
            a.dma_start(stage[0:P, 1, :], taps[0:P]).then_inc(vec_in, 16)
            a.dma_start(stage[0:3 * 2 * FT - P, 2, :], taps[P:3 * 2 * FT]).then_inc(vec_in, 16)
            for e in range(2):
                a.dma_start(w2d[:, :, e, :], cmp_w2[0, 0].rearrange("(h p) d -> p h d", p=P)).then_inc(w2_in, 16)
            a.dma_start(w2v[:, :, :], cmp_w2[0, 1].rearrange("(h p) d -> p h d", p=P)).then_inc(w2_in, 16)
            a.dma_start(w1raw[:, :, :], cmp_w1[0, 0].rearrange("(j p) c -> p j c", p=P)).then_inc(w1_in[0], 16)

            def squares(which, src, ready):
                for t in range(TB):
                    ready(t)
                    a.activation(junk[:, t, :], src[:, t, :], ACT.Square, accum_out=sumsq[:, which, t:t + 1]).then_inc(sq_done, 1)

            junk = xn
            squares(0, xs, lambda t: act_.wait_ge(x_in[t], 16))
            high(N_GATE)

            def hT_high(which, gain):
                for k in range(KT):
                    act_.wait_ge(xT_ready, KT * which + k + 1)
                    a.activation(hT_h[:, k, :], bank[k % 4][:, :], ACT.Copy, scale=vec[:, gain + k:gain + k + 1]).then_inc(hT_h_done, 1)

            act_.wait_ge(vec_done, 3)
            hT_high(0, V_ANORM)
            high(N_CMP)
            high(N_CMP + 1)
            act_.wait_ge(tile_done, N_GATE + 1)
            a.activation(glT[:, :], pj[0][:, :], ACT.Copy).then_inc(glT_done, 1)
            act_.wait_ge(gateT_ready, 1)
            a.activation(gates[:, :, :, :],
                         pj[1][:, :].rearrange("p (i c) -> p i c", c=P)[:, :, GATE_ROW:P].rearrange("p i (h c) -> p h c i", c=3),
                         ACT.Tanh, scale=0.5).then_inc(gate_tanh, 1)
            high(N_CMP + 2)
            high(N_CMP + 3)

            def w1_high(c):
                act_.wait_ge(w1_in[c], 16)
                if c:
                    act_.wait_ge(hid_ready, 1)
                a.activation(w1h[:, :, :], w1raw[:, :, :], ACT.Copy).then_inc(w1h_done, 1)

            w1_high(0)
            act_.wait_ge(const_ready, N_CONST)
            for g in range(GROUPS):
                act_.wait_ge(tile_done, N_CMP + g + 1)
                src = pj[g % 2]
                a.activation(vc2[0:HD, g, 0:T], src[HD:P, :], ACT.Copy).then_inc(c_copied, 1)
                a.activation(vc2[HD:P, g, 0:T - 1], src[HD:P, 1:T], ACT.Copy).then_inc(c_copied, 1)
                high(N_GRP + g)

            for c in range(2):
                if c:
                    w1_high(1)
                act_.wait_ge(gel_step, 4 * c + 3)
                a.activation(gel2[0:GROUPS * NC, :], gel2[0:GROUPS * NC, :], ACT.Tanh, scale=GELU_C).then_inc(gel_tanh, 1)
                if c == 0:
                    act_.wait_ge(w1l_done, 1)
                    a.dma_start(w1raw[:, :, :], cmp_w1[0, 1].rearrange("(j p) c -> p j c", p=P)).then_inc(w1_in[1], 16)
                    act_.wait_ge(cmp_ready, 1)
                    a.activation(kkc_h[:, :, :].rearrange("p g n -> p (g n)"), sc[1][:, 0:GROUPS * NC], ACT.Copy).then_inc(kkch_done, 1)

            def exp_unit(H, r, u):
                i, b = divmod(u, 2)
                n = (i + 1) * P
                par = r % 2
                act_.wait_ge(masked, UNITS * H + u + 1 + C_MASKED)
                p = prob[:, par, b, poff(i):poff(i) + n]
                a.activation(p, p, ACT.Exp, scale=-1.0, bias=mn[:, par, u:u + 1],
                             accum_out=sums[:, par, 1 + b, i:i + 1]).then_inc(exp_done, 1)

            def exp_cmp(H, r):
                act_.wait_ge(c_shifted, H + 1)
                a.activation(sc_c[:, r % 2, :, :], sc_c[:, r % 2, :, :], ACT.Exp, scale=-1.0).then_inc(c_exp, 1)

            def pt_high(H, r, v):
                V = PT_UNITS * H + v
                s = (PT_UNITS * r + v) % 2
                n, rows_ = (T, TB * NC) if v == 0 else (T - P * ((v - 1) % TB), P)
                act_.wait_ge(tr_ready, V + 1 + C_TR)
                act_.wait_ge(av_done, V + 1)
                a.activation(pt_h[0:rows_, s, 0:n], tr[s][0:rows_, 0:n], ACT.Copy).then_inc(pth_done, 1)

            def o_evac(H, g, r):
                half = (r % 2) * HD
                act_.wait_ge(av_done, PT_UNITS * (H + 1) + C_AV)
                a.activation(otmp[half:half + HD, :], ob[HD:P, :], ACT.Copy).then_inc(o_copied, 1)

            def o_high(H, g, r):
                half = (r % 2) * HD
                act_.wait_ge(o_summed, H + 1 + C_O)
                a.activation(oT_h[half:half + HD, bass.ds(2 * g + r // 2, 1), :], osum[half:half + HD, r % 2:r % 2 + 1, :], ACT.Copy)\
                    .then_inc(oh_done, 1)

            def group(g, n_tiles):
                act_.wait_ge(tile_done, 4 * g + N_GRP + 1)
                for b in range(2):
                    src = pj[0][HD * b:HD * b + HD, :]
                    for half in (b, 1 - b):
                        a.activation(kk_h[HD * half:HD * half + HD, b, :], src, ACT.Copy).then_inc(kvh_done, 1)
                act_.wait_ge(tile_done, 4 * g + N_GRP + 2)
                a.activation(vT[:, :], pj[1][:, :], ACT.Copy).then_inc(vT_done, 1)
                act_.wait_ge(gateT_ready, g + 2)
                a.activation(vv[:, :, :, 0, :], pj[0][:, :].rearrange("p (t b d) -> p b t d", t=TB, b=2), ACT.Copy).then_inc(kvh_done, 1)
                for q in range(2):
                    act_.wait_ge(tile_done, 4 * g + N_GRP + 3 + q)
                    for e in range(2):
                        rows_ = slice(HD * e, HD * e + HD)
                        a.activation(qq[rows_, 2 * q + e, :], pj[1 - q][rows_, :], ACT.Copy, scale=-SCALE).then_inc(qh_done, 1)
                for u in range(UNITS):
                    exp_unit(g * R, 0, u)
                exp_cmp(g * R, 0)
                for r in range(R):
                    H = g * R + r
                    for v in range(PT_UNITS):
                        pt_high(H, r, v)
                        if r + 1 < R:
                            if v < UNITS:
                                exp_unit(H + 1, r + 1, v)
                            else:
                                exp_cmp(H + 1, r + 1)
                    o_evac(H, g, r)
                    o_high(H, g, r)
                    high(N_GRP + RING + r, g)

            with act_.Fori(0, GROUPS) as g:
                group(g, None)
            for n in range(N_OUT + RING, N_UP + RING):
                high(n)
            for t in range(TB):
                act_.wait_ge(x1_done, 2 * t + 2)
                a.activation(x1n[:, t, :], xs[:, t, :], ACT.Square, accum_out=sumsq[:, 1, t:t + 1]).then_inc(sq_done, 1)
            hT_high(1, V_MNORM)

            with act_.Fori(0, FT // 2) as i:
                for m in range(2):
                    for h in range(2):
                        j = 2 * m + h
                        act_.wait_ge(tile_done, 4 * i + N_UP + j + 1)
                        act_.wait_ge(act_done, 2 * i + m + 1)
                        col = 2 * i + (m + h * FT)
                        a.activation(conv[:, j, :], bank[j][:, :], ACT.Identity,
                                     scale=vec[:, bass.ds(col + (V_CW + 2 * 2 * FT), 1)], bias=vec[:, bass.ds(col + V_CB, 1)])\
                            .then_inc(conv0, 1)
                        high(N_UP + RING + j, i)
                    act_.wait_ge(conv_done, 4 * i + 2 * m + 2 + C_CONV)
                    a.activation(th[:, m, :], conv[:, 2 * m + 1, :], ACT.Tanh, scale=0.5).then_inc(g_tanh, 1)
                    act_.wait_ge(act_done, 2 * i + m + 1 + C_AH)
                    a.activation(aT_h[:, bass.ds(2 * i + m, 1), :], act[:, m:m + 1, :], ACT.Copy).then_inc(ah_done, 1)
            for n in range(N_DOWN + RING, N_DOWN + 2 + RING):
                high(n)
            with act_.Fori(0, (FT - 2 - RING) // RING) as i:
                for j in range(RING):
                    high(N_DOWN + 2 + RING + j, i)
            a.dma_start(fgain[:, :], final_norm.rearrange("(a d) -> a d", a=1).broadcast_to([P, D])).then_inc(fgain_in, 16)
            for n in range(0, KT, 2):
                act_.wait_ge(yT_ready, n + 1)
                a.activation(yT[:, n, :], bank[n][:, :], ACT.Copy).then_inc(yT_act, 1)
            for t in range(TB):
                act_.wait_ge(x2_done, 2 * t + 2)
                a.activation(raw[:, t, :], xs[:, t, :], ACT.Square, accum_out=sumsq[:, 2, t:t + 1]).then_inc(sq_done, 1)

        @block.vector
        def _(dve):
            v_ = nc.vector
            dve.sem_inc(masked, C_MASKED)
            dve.sem_inc(cc_biased, C_CC)
            dve.sem_inc(pt_done, C_PT)
            dve.sem_inc(o_summed, C_O)
            dve.sem_inc(conv_done, C_CONV)
            dve.sem_inc(act_done, C_AH)

            def normed(which, dst):
                for t in range(TB):
                    dve.wait_ge(rstd_done, TB * which + t + 1)
                    v_.tensor_scalar(dst[:, t, :], xs[:, t, :], rstd[:, which, t:t + 1], None, ALU.mult).then_inc(xn_done, 1)

            def hT_low(which, gain):
                for k in range(KT):
                    dve.wait_ge(hT_h_done, KT * which + k + 1)
                    v_.scalar_tensor_tensor(hT_l[:, k, :], bank[k % 4][:, :], vec[:, gain + k:gain + k + 1],
                                            hT_h[:, k, :].bitcast(F32), ALU.mult, ALU.subtract).then_inc(hT_done, 1)

            for n, (c0, c1) in enumerate(((0, V_A), (V_A, V_A + P), (V_A + P, V_CW + 3 * 2 * FT))):
                dve.wait_ge(vecT_ready, n + 1)
                v_.tensor_copy(vec[:, c0:c1], bank[4 + n][:, 0:c1 - c0]).then_inc(vec_done, 1)
            dve.wait_ge(const_ready, N_CONST)
            for r in range(R):
                s = slopes()[r]
                if r == R - 1:
                    dve.wait_ge(bias_done, 2 * r)
                v_.tensor_scalar(bias[:, r, :], bias[:, R - 1, :], s, None, ALU.mult).then_inc(bias_done, 1)
                v_.tensor_scalar(bias_c[:, r, :, :], bias_c[:, R - 1, :, :], s, None, ALU.mult).then_inc(bias_done, 1)
            normed(0, xn)
            dve.wait_ge(vec_done, 3)
            hT_low(0, V_ANORM)
            dve.wait_ge(gate_tanh, 1)
            v_.tensor_scalar(gates[:, :, :, :], gates[:, :, :, :], 0.5, 0.5, ALU.mult, ALU.add).then_inc(gates_done, 1)
            dve.wait_ge(gates_done, 1)
            v_.tensor_scalar(gates[:, :, 0, 0], gates[:, :, 0, 0], valid[:, 0:1], None, ALU.mult).then_inc(gates_done, 1)

            def w1_low(c):
                dve.wait_ge(w1h_done, c + 1)
                v_.tensor_tensor(w1l[:, :, :], w1raw[:, :, :], w1h[:, :, :].bitcast(F32), ALU.subtract).then_inc(w1l_done, 1)

            w1_low(0)
            for g in range(GROUPS):
                dve.wait_ge(tile_done, N_CMP + g + 1)
                src = pj[g % 2]
                v_.tensor_copy(kc2[0:HD, g, 0:T], src[0:HD, :])
                v_.tensor_copy(kc2[HD:P, g, 0:T - 1], src[0:HD, 1:T]).then_inc(pj_evac, 1)

            nb = GROUPS * NC
            for c, src in enumerate((kc2, vc2)):
                if c:
                    w1_low(1)
                    dve.wait_ge(hid_ready, 1)
                    dve.wait_ge(c_copied, 2 * GROUPS)
                else:
                    dve.wait_ge(pj_evac, GROUPS)
                for j in range(CJ):
                    window = src[:, :, 2 * j:2 * j + STRIDE * (NC - 1) + 1:STRIDE]
                    pos = vec[:, V_POS + c * CJ + j:V_POS + c * CJ + j + 1]
                    v_.tensor_scalar(blk_h[:, j, :, :], window, pos, None, ALU.add).then_inc(blkh_done, 1)
                    dve.wait_ge(blkh_done, c * CJ + j + 1)
                    v_.scalar_tensor_tensor(blk_l[:, j, :, :], window, pos, blk_h[:, j, :, :].bitcast(F32), ALU.add, ALU.subtract)\
                        .then_inc(blk_done, 1)
                hid = sc[0][0:nb, 0:HID]
                dve.wait_ge(hid_ready, c + 1)
                v_.tensor_copy(gel[0:nb, :], hid).then_inc(gel_step, 1)
                dve.wait_ge(gel_step, 4 * c + 1)
                v_.tensor_tensor(gel2[0:nb, :], gel[0:nb, :], gel[0:nb, :], ALU.mult).then_inc(gel_step, 1)
                dve.wait_ge(gel_step, 4 * c + 2)
                v_.tensor_scalar(gel2[0:nb, :], gel2[0:nb, :], 0.044715, 1.0, ALU.mult, ALU.add).then_inc(gel_mid, 1)
                dve.wait_ge(gel_mid, 2 * c + 1)
                v_.tensor_tensor(gel2[0:nb, :], gel2[0:nb, :], gel[0:nb, :], ALU.mult).then_inc(gel_step, 1)
                dve.wait_ge(gel_tanh, c + 1)
                v_.tensor_scalar(gel2[0:nb, :], gel2[0:nb, :], 0.5, 0.5, ALU.mult, ALU.add).then_inc(gel_mid, 1)
                dve.wait_ge(gel_mid, 2 * c + 2)
                v_.tensor_tensor(gel[0:nb, :], gel2[0:nb, :], gel[0:nb, :], ALU.mult).then_inc(gel_step, 1)
                dve.wait_ge(gelT_ready, c + 1)
                if c == 0:
                    v_.tensor_copy(gT[:, :, :], cc[:, 0:2 * nb].rearrange("p (a n) -> p a n", a=2)).then_inc(gT_done, 1)
                    dve.wait_ge(kkch_done, 1)
                    v_.tensor_tensor(kkc_l[:, :, :].rearrange("p g n -> p (g n)"), sc[1][:, 0:nb],
                                     kkc_h[:, :, :].rearrange("p g n -> p (g n)").bitcast(F32), ALU.subtract).then_inc(cmp_done, 1)
                else:
                    for rep in range(TB):
                        v_.tensor_copy(gTr[:, :, :, rep, :], cc[:, 0:2 * nb].rearrange("p (a g n) -> p g a n", a=2, g=GROUPS)).then_inc(gT_done, 1)
                    dve.wait_ge(cmp_ready, 2)
                    v_.tensor_copy(vvc_all[:, :, :], sc[1][:, 0:GROUPS * HD].rearrange("p (g d) -> p g d", g=GROUPS)).then_inc(cmp_done, 1)
            v_.memset(pbd[:, :, :, :, :].rearrange("p a b c n -> p (a b c n)"), 0.0).then_inc(gel_mid, 1)
            dve.wait_ge(gel_mid, 5)

            def mask_unit(H, r, u):
                i, b = divmod(u, 2)
                n = (i + 1) * P
                par = r % 2
                U = UNITS * H + u
                dve.wait_ge(scores_ready, U + 1)
                dve.sem_inc(mask_begun, 1)
                v_.tensor_tensor_reduce(prob[:, par, b, poff(i):poff(i) + n], sc[u % 2][:, 0:n], bias[:, r, T - n:T], 1.0, MASKED * 10,
                                        ALU.add, ALU.min, mn[:, par, u:u + 1]).then_inc(masked, 1)

            def mask_cmp(H, r):
                par = r % 2
                dve.wait_ge(cc_ready, H + 1)
                s = sc_c[:, par, :, :]
                v_.tensor_tensor(s, cc[:, 0:TB * NC].rearrange("p (i n) -> p i n", i=TB), bias_c[:, r, :, :], ALU.add).then_inc(cc_biased, 1)
                dve.wait_ge(cc_biased, H + 1 + C_CC)
                v_.tensor_reduce(mn_c[:, par, :], s, AX, ALU.min).then_inc(c_min, 1)
                dve.wait_ge(c_min, H + 1)
                v_.tensor_tensor(s, s, mn_c[:, par, :].unsqueeze(2).broadcast_to([P, TB, NC]), ALU.subtract).then_inc(c_shifted, 1)

            def normalise(g, H, r):
                par = r % 2
                dve.wait_ge(c_exp, H + 1)
                s = sc_c[:, par, :, :]
                v_.tensor_reduce(sums[:, par, 0, :], s, AX, ALU.add).then_inc(c_sum, 1)
                dve.wait_ge(c_sum, H + 1)
                dve.wait_ge(exp_done, UNITS * (H + 1))
                v_.reciprocal(rs[:, par, :, :], sums[:, par, :, :]).then_inc(recip_done, 1)
                dve.wait_ge(recip_done, H + 1)
                v_.tensor_tensor(rs[:, par, :, :], rs[:, par, :, :], gates[:, bass.ds(H, 1), :, :].rearrange("p a c i -> p (a c) i"), ALU.mult)\
                    .then_inc(rs_done, 1)
                dve.wait_ge(rs_done, H + 1)
                diag = pbd[:, par, :, :, :].rearrange("p i j n -> p (i j) n")[:, 0:TB * TB:TB + 1, :]
                v_.tensor_tensor(diag, s, rs[:, par, 0, :].unsqueeze(2).broadcast_to([P, TB, NC]), ALU.mult).then_inc(p_ready, 1)
                for b in range(2):
                    for i in range(TB):
                        p = prob[:, par, b, poff(i):poff(i) + (i + 1) * P]
                        v_.tensor_scalar(p, p, rs[:, par, 1 + b, i:i + 1], None, ALU.mult).then_inc(p_ready, 1)

            def pt_low(H, r, v):
                V = PT_UNITS * H + v
                s = (PT_UNITS * r + v) % 2
                n, rows_ = (T, TB * NC) if v == 0 else (T - P * ((v - 1) % TB), P)
                dve.wait_ge(pth_done, V + 1)
                v_.tensor_tensor(pt_l[0:rows_, s, 0:n], tr[s][0:rows_, 0:n], pt_h[0:rows_, s, 0:n].bitcast(F32), ALU.subtract).then_inc(pt_done, 1)

            def o_sum(H, g, r):
                half = (r % 2) * HD
                dve.wait_ge(o_copied, H + 1)
                v_.tensor_tensor(osum[half:half + HD, r % 2, :], ob[0:HD, :], otmp[half:half + HD, :], ALU.add).then_inc(o_summed, 1)

            def o_low(H, g, r):
                half = (r % 2) * HD
                dve.wait_ge(oh_done, H + 1)
                dst = (slice(half, half + HD), bass.ds(2 * g + r // 2, 1), slice(None))
                v_.tensor_tensor(oT_l[dst], osum[half:half + HD, r % 2:r % 2 + 1, :], oT_h[dst].bitcast(F32), ALU.subtract).then_inc(oT_done, 1)

            def rescale(H, r):
                dve.wait_ge(masked, UNITS * (H + 1) + C_MASKED)
                v_.tensor_scalar(bias[:, r, :], bias[:, r, :], SLOPE_STEP, None, ALU.mult).then_inc(bias_done, 1)
                v_.tensor_scalar(bias_c[:, r, :, :], bias_c[:, r, :, :], SLOPE_STEP, None, ALU.mult).then_inc(bias_done, 1)

            def group(g):
                dve.wait_ge(cmp_done, 2)
                v_.tensor_copy(vvc[0:nb, 0:1, :], vvc_all[0:nb, bass.ds(g, 1), :]).then_inc(vvc_done, 1)
                dve.wait_ge(vvc_done, 2 * g + 1)
                v_.tensor_tensor(vvc[0:nb, 1:2, :], vvc_all[0:nb, bass.ds(g, 1), :], vvc[0:nb, 0:1, :].bitcast(F32), ALU.subtract).then_inc(vvc_done, 1)
                dve.wait_ge(kvh_done, 5 * g + 4)
                for b in range(2):
                    same, other = slice(HD * b, HD * b + HD), slice(HD - HD * b, P - HD * b)
                    for dst in (same, other):
                        m = v_.tensor_tensor(kk_l[dst, b, :], pj[0][same, :], kk_h[same, b, :].bitcast(F32), ALU.subtract)
                m.then_inc(pj_evac, 1)
                dve.wait_ge(kvh_done, 5 * g + 5)
                v_.tensor_tensor(vv[:, :, :, 1, :], pj[0][:, :].rearrange("p (t b d) -> p b t d", t=TB, b=2), vv[:, :, :, 0, :].bitcast(F32), ALU.subtract)\
                    .then_inc(pj_evac, 1)
                for q in range(2):
                    for e in range(2):
                        rows_, other = slice(HD * e, HD * e + HD), slice(HD - HD * e, P - HD * e)
                        dve.wait_ge(qh_done, 4 * g + 2 * q + e + 1)
                        m = v_.scalar_tensor_tensor(qq[other, 2 * q + e, :], pj[1 - q][rows_, :], -SCALE, qq[rows_, 2 * q + e, :].bitcast(F32),
                                                    ALU.mult, ALU.subtract)
                    m.then_inc(pj_evac, 1)
                dve.wait_ge(bias_done, 2 * R * g + 2 * R)
                dve.wait_ge(tr_ready, PT_UNITS * (g * R) - PT_UNITS + C_TR)
                for u in range(UNITS):
                    mask_unit(g * R, 0, u)
                mask_cmp(g * R, 0)
                for r in range(R):
                    H = g * R + r
                    normalise(g, H, r)
                    rescale(H, r)
                    if r + 1 < R:
                        dve.wait_ge(tr_ready, PT_UNITS * H + C_TR)
                    for v in range(PT_UNITS):
                        pt_low(H, r, v)
                        if r + 1 < R:
                            if v < UNITS:
                                mask_unit(H + 1, r + 1, v)
                            else:
                                mask_cmp(H + 1, r + 1)
                    o_sum(H, g, r)
                    o_low(H, g, r)

            with dve.Fori(0, GROUPS) as g:
                group(g)

            for t in range(TB):
                for h in range(2):
                    if 2 * t + h < 2 * TB - 1:
                        dve.wait_ge(y_ready, 2 * t + h + 1)
                    else:
                        dve.wait_ge(tile_done, N_UP)
                    cols_ = slice(512 * h, 512 * h + 512)
                    v_.tensor_tensor(xs[:, t, cols_], bank[2 * t + h][:, :], xs[:, t, cols_], ALU.add).then_inc(x1_done, 1)
            normed(1, x1n)
            hT_low(1, V_MNORM)

            with dve.Fori(0, FT // 2) as i:
                for m in range(2):
                    for h in range(2):
                        j = 2 * m + h
                        for tap, back in ((1, 1), (0, 2)):
                            dve.wait_ge(conv0 if tap else conv1, 4 * i + j + 1)
                            col = 2 * i + (m + h * FT + V_CW + tap * 2 * FT)
                            v_.scalar_tensor_tensor(conv[:, j, back:T], bank[j][:, 0:T - back], vec[:, bass.ds(col, 1)], conv[:, j, back:T],
                                                    ALU.mult, ALU.add).then_inc(conv1 if tap else conv_done, 1)
                    dve.wait_ge(g_tanh, 2 * i + m + 1)
                    v_.scalar_tensor_tensor(th[:, m, :], th[:, m, :], 1.0, conv[:, 2 * m + 1, :], ALU.add, ALU.mult).then_inc(silu_done, 1)
                    dve.wait_ge(silu_done, 2 * i + m + 1)
                    v_.scalar_tensor_tensor(act[:, m, :], th[:, m, :], 0.5, conv[:, 2 * m, :], ALU.mult, ALU.mult).then_inc(act_done, 1)
                    dve.wait_ge(ah_done, 2 * i + m + 1)
                    v_.tensor_tensor(aT_l[:, bass.ds(2 * i + m, 1), :], act[:, m:m + 1, :], aT_h[:, bass.ds(2 * i + m, 1), :].bitcast(F32),
                                     ALU.subtract).then_inc(aT_done, 1)
            for n in range(1, KT, 2):
                dve.wait_ge(yT_ready, n + 1)
                v_.tensor_copy(yT[:, n, :], bank[n][:, :]).then_inc(yT_dve, 1)
            for t in range(TB):
                for h in range(2):
                    dve.wait_ge(z_ready, 2 * t + h + 1)
                    cols_ = slice(512 * h, 512 * h + 512)
                    v_.tensor_tensor(xs[:, t, cols_], bank[2 * t + h][:, :], xs[:, t, cols_], ALU.add).then_inc(x2_done, 1)
            dve.wait_ge(fgain_in, 16)
            for t in range(TB):
                dve.wait_ge(rstd_done, 2 * TB + t + 1)
                v_.scalar_tensor_tensor(xs[:, t, :], xs[:, t, :], rstd[:, 2, t:t + 1], fgain[:, :], ALU.mult, ALU.mult).then_inc(out_done, 1)

        @block.tensor
        def _(pe):
            t_ = nc.tensor
            pe.sem_inc(tr_ready, C_TR)
            pe.sem_inc(av_done, C_AV)

            def xT(which, src, gain):
                for k in range(KT):
                    if k == 0:
                        pe.wait_ge(xn_done, TB * which + TB)
                    if k >= 4:
                        pe.wait_ge(hT_done, KT * which + k - 3)
                    for t in range(TB):
                        m = t_.transpose(bank[k % 4][:, t * P:(t + 1) * P], src[:, t, k * P:(k + 1) * P], ident[:, :])
                    m.then_inc(xT_ready, 1)

            def tile_ready(n, more=None):
                pe.wait_ge(wl_done, n + 1 if more is None else n + 1 + RING * more)

            def project(n, dst, more=None):
                tile_ready(n, more)
                s = slot(n)
                for k in range(KT):
                    c = slice(k * P, (k + 1) * P)
                    t_.matmul(dst[:, :], wh[:, s, c], hT_h[:, k, :], start=(k == 0), stop=False)
                    t_.matmul(dst[:, :], wh[:, s, c], hT_l[:, k, :], start=False, stop=False)
                    m = t_.matmul(dst[:, :], wl[:, s, c], hT_h[:, k, :], start=False, stop=(k == KT - 1))
                m.then_inc(tile_done, 1)

            pe.wait_ge(vec_in, 16 * 6)
            pe.wait_ge(const_ready, 3)
            for n in range(3):
                t_.transpose(bank[4 + n][:, 0:P], stage[:, n, :], ident[:, :]).then_inc(vecT_ready, 1)
            xT(0, xn, V_ANORM)
            pe.wait_ge(hT_done, KT)
            project(N_GATE, pj[0])
            pe.wait_ge(glT_done, 1)
            for t in range(TB):
                m = t_.transpose(pj[1][:, t * P:(t + 1) * P], glT[:, t * P:(t + 1) * P], ident[:, :])
            m.then_inc(gateT_ready, 1)
            for g in range(GROUPS):
                if g == 1:
                    pe.wait_ge(gate_tanh, 1)
                if g >= 2:
                    pe.wait_ge(pj_evac, g - 1)
                    pe.wait_ge(c_copied, 2 * (g - 1))
                project(N_CMP + g, pj[g % 2])

            nb = GROUPS * NC
            pe.wait_ge(w2_in, 48)
            for c in range(2):
                pe.wait_ge(w1l_done, c + 1)
                for j in range(CJ):
                    pe.wait_ge(blk_done, c * CJ + j + 1)
                    bh = blk_h[:, j, :, :].rearrange("p g n -> p (g n)")
                    bl = blk_l[:, j, :, :].rearrange("p g n -> p (g n)")
                    dst = sc[0][0:nb, 0:HID]
                    if c and j == 0:
                        pe.wait_ge(gel_step, 4)
                    t_.matmul(dst, bh, w1h[:, j, :], start=(j == 0), stop=False)
                    t_.matmul(dst, bh, w1l[:, j, :], start=False, stop=False)
                    m = t_.matmul(dst, bl, w1h[:, j, :], start=False, stop=(j == CJ - 1))
                m.then_inc(hid_ready, 1)
                pe.wait_ge(gel_step, 4 * c + 4)
                for h in range(2):
                    m = t_.transpose(cc[:, h * nb:h * nb + nb], gel[0:nb, h * P:(h + 1) * P], ident[0:nb, 0:nb])
                m.then_inc(gelT_ready, 1)
                pe.wait_ge(gT_done, TB * c + 1)
                if c == 0:
                    for h in range(2):
                        m = t_.matmul(sc[1][:, 0:nb], w2d[:, h, :, :].rearrange("p e d -> p (e d)"), gT[:, h, :], start=(h == 0), stop=(h == 1))
                    m.then_inc(cmp_ready, 1)
                else:
                    pe.wait_ge(cmp_done, 1)
                    for g in range(GROUPS):
                        for h in range(2):
                            m = t_.matmul(sc[1][0:nb, g * HD:(g + 1) * HD], gTr[:, g, h, :, :].rearrange("p r n -> p (r n)"), w2v[:, h, :], start=(h == 0), stop=(h == 1))
                    m.then_inc(cmp_ready, 1)

            def score_unit(H, r, u):
                i, b = divmod(u, 2)
                n = (i + 1) * P
                pe.wait_ge(masked, UNITS * H + u + 1)
                q = qq[:, r, i * P:(i + 1) * P]
                t_.matmul(sc[u % 2][:, 0:n], q, kk_h[:, b, 0:n], start=True, stop=False)
                t_.matmul(sc[u % 2][:, 0:n], q, kk_l[:, b, 0:n], start=False, stop=True).then_inc(scores_ready, 1)

            def score_cmp(H, g, r):
                pe.wait_ge(cc_biased, H + 1)
                kh, kl = (z[:, bass.ds(g, 1), :].rearrange("p a n -> p (a n)") for z in (kkc_h, kkc_l))
                for i in range(TB):
                    q = qq[:, r, i * P:(i + 1) * P]
                    dst = cc[:, i * NC:(i + 1) * NC]
                    t_.matmul(dst, q, kh, start=True, stop=False)
                    m = t_.matmul(dst, q, kl, start=False, stop=True)
                m.then_inc(cc_ready, 1)

            def transpose_unit(H, r, v):
                V = PT_UNITS * H + v
                s = (PT_UNITS * r + v) % 2
                par = r % 2
                pe.wait_ge(pt_done, V + 1)
                if v == 0:
                    pe.wait_ge(p_ready, PT_UNITS * H + 1)
                    for i in range(TB):
                        m = t_.transpose(tr[s][0:TB * NC, i * P:(i + 1) * P], pbd[:, par, i, :, :].rearrange("p j n -> p (j n)"), ident[:, :])
                else:
                    b, j = divmod(v - 1, TB)
                    pe.wait_ge(p_ready, PT_UNITS * H + 1 + TB * (b + 1))
                    for i in range(j, TB):
                        m = t_.transpose(tr[s][:, (i - j) * P:(i - j + 1) * P], prob[:, par, b, poff(i) + j * P:poff(i) + (j + 1) * P], ident[:, :])
                m.then_inc(tr_ready, 1)

            def av_unit(H, r, v):
                V = PT_UNITS * H + v
                s = (PT_UNITS * r + v) % 2
                if v == 0:
                    pe.wait_ge(o_summed, H + 1)
                pe.wait_ge(pt_done, V + 1 + C_PT)
                if v == 0:
                    w, rows_, n = vvc[0:TB * NC, :, :].rearrange("p a d -> p (a d)"), TB * NC, T
                else:
                    b, j = divmod(v - 1, TB)
                    w, rows_, n = vv[:, b, j, :, :].rearrange("p a d -> p (a d)"), P, T - j * P
                dst = ob[:, T - n:T]
                t_.matmul(dst, w, pt_h[0:rows_, s, 0:n], start=(v == 0), stop=False)
                t_.matmul(dst, w, pt_l[0:rows_, s, 0:n], start=False, stop=(v == PT_UNITS - 1)).then_inc(av_done, 1)

            def group(g):
                pe.wait_ge(pj_evac, 4 * g + GROUPS)
                project(N_GRP, pj[0], g)
                project(N_GRP + 1, pj[1], g)
                pe.wait_ge(vT_done, g + 1)
                pe.wait_ge(pj_evac, 4 * g + 1 + GROUPS)
                for t in range(TB):
                    m = t_.transpose(pj[0][:, t * P:(t + 1) * P], vT[:, t * P:(t + 1) * P], ident[:, :])
                m.then_inc(gateT_ready, 1)
                project(N_GRP + 2, pj[1], g)
                pe.wait_ge(pj_evac, 4 * g + 2 + GROUPS)
                project(N_GRP + 3, pj[0], g)
                pe.wait_ge(pj_evac, 4 * g + 4 + GROUPS)
                pe.wait_ge(vvc_done, 2 * g + 2)
                for u in range(UNITS):
                    score_unit(g * R, 0, u)
                score_cmp(g * R, g, 0)
                for r in range(R):
                    H = g * R + r
                    transpose_unit(H, r, 0)
                    for v in range(PT_UNITS):
                        if r + 1 < R:
                            if v < UNITS:
                                score_unit(H + 1, r + 1, v)
                            else:
                                score_cmp(H + 1, g, r + 1)
                        if v + 1 < PT_UNITS:
                            transpose_unit(H, r, v + 1)
                        av_unit(H, r, v)

            with pe.Fori(0, GROUPS) as g:
                group(g)

            pe.wait_ge(oT_done, HEADS)
            pe.wait_ge(masked, UNITS * HEADS + C_MASKED)
            for k in range(KT):
                n = N_OUT + k
                tile_ready(n)
                s = slot(n)
                for t in range(TB):
                    tc = slice(t * P, (t + 1) * P)
                    for o, w in ((oT_h, wh), (oT_h, wl), (oT_l, wh)):
                        for h in range(2):
                            m = t_.matmul(bank[2 * t + h][:, :], o[:, k, tc], w[:, s, 512 * h:512 * h + 512],
                                          start=(k == 0 and o is oT_h and w is wh), stop=(k == KT - 1 and o is oT_l))
                            if k == KT - 1 and o is oT_l and 2 * t + h < 2 * TB - 1:
                                m.then_inc(y_ready, 1)
                m.then_inc(tile_done, 1)
            pe.wait_ge(x1_done, 2 * TB)
            xT(1, x1n, V_MNORM)
            pe.wait_ge(hT_done, 2 * KT)

            with pe.Fori(0, FT // 2) as i:
                for j in range(RING):
                    pe.wait_ge(conv_done, 4 * i + j + 1)
                    project(N_UP + j, bank[j], i)

            pe.wait_ge(conv_done, 2 * FT + C_CONV)

            def down(k, n, more=None, last=False):
                pe.wait_ge(aT_done, k + 1)
                tile_ready(n, more)
                s = slot(n)
                first = more is None and n == N_DOWN
                ah, al = aT_h[:, bass.ds(k, 1), :], aT_l[:, bass.ds(k, 1), :]
                ah, al = (z.rearrange("p a t -> p (a t)") for z in (ah, al))
                for c in range(KT):
                    cs = slice(c * P, (c + 1) * P)
                    t_.matmul(bank[c][:, :], wh[:, s, cs], ah, start=first, stop=False, skip_group_check=True)
                    t_.matmul(bank[c][:, :], wh[:, s, cs], al, start=False, stop=False, skip_group_check=True)
                    m = t_.matmul(bank[c][:, :], wl[:, s, cs], ah, start=False, stop=last, skip_group_check=True)
                    if last:
                        m.then_inc(yT_ready, 1)
                if not last:
                    m.then_inc(tile_done, 1)

            for k in range(2):
                down(k, N_DOWN + k)
            with pe.Fori(0, (FT - 2 - RING) // RING) as i:
                for j in range(RING):
                    down(i * RING + (2 + j), N_DOWN + 2 + j, i)
            for k in range(FT - RING, FT):
                down(k, N_DOWN + k, None, k == FT - 1)
            pe.wait_ge(yT_act, KT // 2)
            pe.wait_ge(yT_dve, KT // 2)
            for t in range(TB):
                for h in range(2):
                    for c in range(4):
                        m = t_.transpose(bank[2 * t + h][:, c * P:(c + 1) * P], yT[:, 4 * h + c, t * P:(t + 1) * P], ident[:, :])
                    m.then_inc(z_ready, 1)


_INS = ['x', 'attn_norm', 'mlp_norm', 'final_norm', 'nsa_w_in', 'nsa_cmp_pos', 'nsa_cmp_w1', 'nsa_cmp_w2', 'nsa_w_out',
        'mlp_w_up', 'mlp_conv_w', 'mlp_conv_b', 'mlp_w_down']


def kernel(**inputs):
    import numpy as _np
    import concourse.bacc as _bacc
    from concourse import mybir as _mybir
    from concourse.bass_utils import run_bass_kernel_spmd as _run

    nc = _bacc.Bacc("TRN2", target_bir_lowering=False, num_devices=1, dynamic_dma_scratch_size=1024)
    arrays, args = {}, []
    for name in _INS:
        a = _np.ascontiguousarray(inputs[name])
        arrays[f"in_{name}"] = a
        args.append(nc.dram_tensor(f"in_{name}", a.shape, _mybir.dt.from_np(a.dtype), kind="ExternalInput").ap())
    args.append(nc.dram_tensor("out_x", (1, T, D), F32, kind="ExternalOutput").ap())
    build(nc, *args)
    r = _run(nc, [arrays], core_ids=[0])
    return r.results[0]["out_x"]
```

```python
from contextlib import ExitStack

import concourse.bass as bass
from concourse import mybir

F32 = mybir.dt.float32
F32R = mybir.dt.float32r
ALU = mybir.AluOpType
ACT = mybir.ActivationFunctionType
AX = mybir.AxisListType.X

P = 128
T = 512
D = 1024
TB = T // P
KT = D // P
HD = 64
HEADS = D // HD
GROUPS = 4
R = HEADS // GROUPS
KV = GROUPS * HD
COL_KC, COL_VC, COL_KS, COL_VS, COL_KW, COL_VW, COL_GATE = (D + n * KV for n in range(7))
W_IN = COL_GATE + 3 * HEADS
COL_GATE_TILE = W_IN - P
GATE_ROW = P - 3 * HEADS
CMP, STRIDE = 32, 16
NC = T // STRIDE
TP = T + CMP // 2
CJ = CMP * HD // P
HID = 256
FF = 2816
FT = FF // P
EPS = 1e-6
SCALE = HD ** -0.5
MASKED = 1e32
GELU_C = 0.7978845608028654
SLOPE_STEP = 2.0 ** (-8.0 * R / HEADS)

RING = 4
N_GATE = 0
N_CMP = 1
N_GRP = N_CMP + GROUPS
N_OUT = N_GRP + 4 * GROUPS
N_UP = N_OUT + KT
N_DOWN = N_UP + 2 * FT
N_END = N_DOWN + FT
UNITS = 2 * TB + 1
STEPS = R * UNITS
AHEAD = 14
BEHIND = 3
SC_RING, TR_RING, PT_RING = 2, 3, 4
V_ANORM, V_MNORM, V_POS, V_CB = 0, KT, 2 * KT, 2 * KT + 2 * CJ
V_A = V_CB + 2 * FT
V_CW = V_A
N_CONST = 11


def slot(n):
    return (n + 3) % RING


def slopes():
    return [2.0 ** (-8.0 * (r + 1) / HEADS) for r in range(R)]


def poff(i):
    return P * i * (i + 1) // 2


def unit_cols(w):
    u = w % UNITS
    return T if u == UNITS - 1 else T - P * (u % TB)


def build(nc, x, attn_norm, mlp_norm, final_norm, nsa_w_in, cmp_pos, cmp_w1, cmp_w2, nsa_w_out, mlp_w_up, conv_w, conv_b, mlp_w_down, out):
    ctx = ExitStack()
    w_in, w_out, w_up, w_down = (w[0] for w in (nsa_w_in, nsa_w_out, mlp_w_up, mlp_w_down))
    with ctx:
        place = {"at": (nc.sbuf_base + 31) // 32 * 32}

        def sb(name, shape, dt=F32, at=None):
            size = 4
            for s in shape[1:]:
                size *= s
            off = place["at"] if at is None else at
            if at is None:
                place["at"] = off + (size + 31) // 32 * 32
            assert off + size <= nc.sbuf_usable_end, (name, off + size)
            return nc.alloc_sbuf_tensor_at(name, shape, dt, offset=off), off + (size + 31) // 32 * 32

        def keep(name, shape, dt=F32):
            return sb(name, shape, dt)[0]

        def sem(name):
            return ctx.enter_context(nc.semaphore(name))

        ident = keep("ident", [P, P])
        vec = keep("vec", [P, V_CW + 3 * 2 * FT])
        half_pow = keep("half_pow", [P, TB])
        sumsq = keep("sumsq", [P, 3, TB])
        meansq = keep("meansq", [P, 3, TB])
        rstd = keep("rstd", [P, 3, TB])
        gates = keep("gates", [P, HEADS, 3, TB])
        valid = keep("valid", [P, 1])
        bias = keep("bias", [P, R, T])
        bias_c = keep("bias_c", [P, R, TB, NC])
        kkc_h = keep("kkc_h", [P, GROUPS, NC], F32R)
        kkc_l = keep("kkc_l", [P, GROUPS, NC], F32R)
        vvc_all = keep("vvc_all", [P, GROUPS, HD])
        xs = keep("xs", [P, TB, D])
        hT_h = keep("hT_h", [P, KT, T], F32R)
        hT_l = keep("hT_l", [P, KT, T], F32R)
        raw = keep("raw", [P, RING, D])
        wh = keep("wh", [P, RING, D], F32R)
        wl = keep("wl", [P, RING, D], F32R)
        base = place["at"]

        def region(specs, at=base):
            made = []
            for name, shape, dt in specs:
                t, at = sb(name, shape, dt, at=at)
                made.append(t)
            return made

        stage, xn, = region([("stage", [P, 3, P], F32), ("xn", [P, TB, D], F32)])
        w1raw, w1h, w1l, kc2, vc2, blk_h, blk_l, gel, gel2, gT, gTr, w2d, w2v, glT = region([
            ("w1raw", [P, CJ, HID], F32), ("w1h", [P, CJ, HID], F32R), ("w1l", [P, CJ, HID], F32R),
            ("kc2", [P, GROUPS, TP], F32), ("vc2", [P, GROUPS, TP], F32),
            ("blk_h", [P, CJ, GROUPS, NC], F32R), ("blk_l", [P, CJ, GROUPS, NC], F32R),
            ("gel", [P, HID], F32), ("gel2", [P, HID], F32), ("gT", [P, 2, GROUPS * NC], F32),
            ("gTr", [P, GROUPS, 2, TB, NC], F32), ("w2d", [P, 2, 2, HD], F32), ("w2v", [P, 2, HD], F32),
            ("glT", [P, T], F32)], at=base + 3 * P * 4 + TB * D * 4)
        (qq, kk_h, kk_l, vv, vvc, prob, sc_c, pbd, pt_h, pt_l, mn, mn_c, sums, rs, vT, otmp, osum, oT_h, oT_l) = region([
            ("qq", [P, R, T], F32R), ("kk_h", [P, 2, T], F32R), ("kk_l", [P, 2, T], F32R),
            ("vv", [P, 2, TB, 2, HD], F32R), ("vvc", [P, 2, HD], F32R),
            ("prob", [P, 2, 2, poff(TB)], F32), ("sc_c", [P, 2, TB, NC], F32), ("pbd", [P, 2, TB, TB, NC], F32),
            ("pt_h", [P, PT_RING, T], F32R), ("pt_l", [P, PT_RING, T], F32R),
            ("mn", [P, 2, 2 * TB], F32), ("mn_c", [P, 2, TB], F32), ("sums", [P, 2, 3, TB], F32), ("rs", [P, 2, 3, TB], F32),
            ("vT", [P, T], F32), ("otmp", [P, T], F32), ("osum", [P, 2, T], F32),
            ("oT_h", [P, KT, T], F32R), ("oT_l", [P, KT, T], F32R)])
        aT_h, aT_l, conv, th, act, fgain = region([
            ("aT_h", [P, FT, T], F32R), ("aT_l", [P, FT, T], F32R),
            ("conv", [P, RING, T], F32), ("th", [P, 2, T], F32), ("act", [P, 2, T], F32), ("fgain", [P, D], F32)],
            at=base)
        x1n, = region([("x1n", [P, TB, D], F32)], at=base)
        yT, = region([("yT", [P, KT, T], F32)], at=base)

        bank = [ctx.enter_context(nc.psum_tensor(f"bank{n}", [P, 512], F32)) for n in range(8)]
        pj = bank[0:2]
        sc = bank[2:4]
        tr = bank[4:7]
        cc, ob = bank[6], bank[7]

        x_in = [sem(f"x_in{t}") for t in range(TB)]
        vec_in = sem("vec_in")
        w1_in = [sem(f"w1_in{c}") for c in range(2)]
        w2_in = sem("w2_in")
        raw_in = [sem(f"raw_in{s}") for s in range(RING)]
        fgain_in = sem("fgain_in")
        stored = sem("stored")
        const_ready = sem("const_ready")
        stage_clear = sem("stage_clear")
        wh_done, wl_done, tile_done = sem("wh_done"), sem("wl_done"), sem("tile_done")
        sq_done, rstd_done, xn_done = sem("sq_done"), sem("rstd_done"), sem("xn_done")
        vecT_ready, vec_done = sem("vecT_ready"), sem("vec_done")
        xT_ready, hT_h_done, hT_done = sem("xT_ready"), sem("hT_h_done"), sem("hT_done")
        pj_evac = sem("pj_evac")
        glT_done, gateT_ready, gate_tanh, gates_done = sem("glT_done"), sem("gateT_ready"), sem("gate_tanh"), sem("gates_done")
        c_copied = sem("c_copied")
        w1h_done, w1l_done, blkh_done, blk_done = sem("w1h_done"), sem("w1l_done"), sem("blkh_done"), sem("blk_done")
        hid_ready, gel_step, gel_tanh, gelT_ready, gT_done = sem("hid_ready"), sem("gel_step"), sem("gel_tanh"), sem("gelT_ready"), sem("gT_done")
        cmp_ready, kkch_done, cmp_done = sem("cmp_ready"), sem("kkch_done"), sem("cmp_done")
        bias_done = sem("bias_done")
        kvh_done, vT_done, gel_mid = sem("kvh_done"), sem("vT_done"), sem("gel_mid")
        vvc_done = sem("vvc_done")
        qh_done = sem("qh_done")
        scores_ready, masked, exp_done = sem("scores_ready"), sem("masked"), sem("exp_done")
        c_min, c_shifted, c_exp, c_sum = sem("c_min"), sem("c_shifted"), sem("c_exp"), sem("c_sum")
        recip_done, rs_done, p_scaled, diag_done = sem("recip_done"), sem("rs_done"), sem("p_scaled"), sem("diag_done")
        tr_ready, pth_done, pt_done, av_done = sem("tr_ready"), sem("pth_done"), sem("pt_done"), sem("av_done")
        o_copied, o_summed, oh_done, oT_done = sem("o_copied"), sem("o_summed"), sem("oh_done"), sem("oT_done")
        mask_begun, scale_begun = sem("mask_begun"), sem("scale_begun")
        y_ready, x1_done = sem("y_ready"), sem("x1_done")
        conv0, conv1, conv_done = sem("conv0"), sem("conv1"), sem("conv_done")
        g_tanh, silu_done, act_done, ah_done, aT_done = sem("g_tanh"), sem("silu_done"), sem("act_done"), sem("ah_done"), sem("aT_done")
        yT_ready, yT_act, yT_dve, z_ready, x2_done = sem("yT_ready"), sem("yT_act"), sem("yT_dve"), sem("z_ready"), sem("x2_done")
        out_done = sem("out_done")
        C_MASKED = SC_RING
        C_TR = 2 * UNITS
        C_PT = TR_RING
        C_AV = PT_RING
        C_O = 1
        C_CONV = RING
        C_AH = 2

        block = ctx.enter_context(nc.Block())

        def stream_wait(eng, n, m4=None):
            s, k = slot(n), (n + 3) // RING + (slot(n) == 3)
            eng.wait_ge(raw_in[s], 32 * k if m4 is None else 32 * (m4 + k))

        @block.sync
        def _(sp):
            def tile_dma(n, halves, more=None):
                s = slot(n)
                if n >= RING:
                    sp.wait_ge(wl_done, n - RING + 1 if more is None else n - RING + 1 + RING * more)
                for dst, src in halves:
                    sp.dma_start(dst, src).then_inc(raw_in[s], 16)

            def cols(w, s, c0, width=P, at=0):
                src = w.rearrange("(k p) c -> p k c", p=P)
                dst = raw[:, s, :].rearrange("p (k c) -> p k c", c=P)
                return [(dst[:, 4 * h:4 * h + 4, at:at + width], src[:, 4 * h:4 * h + 4, bass.ds(c0, width)]) for h in range(2)]

            def pair(w, s, c0, c1):
                src = w.rearrange("(k p) c -> p k c", p=P)
                dst = raw[:, s, :].rearrange("p (k c) -> p k c", c=P)
                return [(dst[:, :, HD * h:HD * h + HD], src[:, :, bass.ds(c, HD)]) for h, c in enumerate((c0, c1))]

            def rows(w, s, r0):
                return [(raw[:, s, 512 * h:512 * h + 512], w[bass.ds(r0, P), 512 * h:512 * h + 512]) for h in range(2)]

            for t in range(TB):
                sp.dma_start(xs[:, t, :], x[0, t * P:(t + 1) * P, :]).then_inc(x_in[t], 16)
            tile_dma(N_GATE, cols(w_in, slot(N_GATE), COL_GATE_TILE))
            for g in range(GROUPS):
                tile_dma(N_CMP + g, pair(w_in, slot(N_CMP + g), COL_KC + HD * g, COL_VC + HD * g))

            with sp.Fori(0, GROUPS) as g:
                tile_dma(N_GRP, cols(w_in, slot(N_GRP), g * R * HD), g)
                tile_dma(N_GRP + 1, pair(w_in, slot(N_GRP + 1), COL_KS + g * HD, COL_KW + g * HD), g)
                tile_dma(N_GRP + 2, pair(w_in, slot(N_GRP + 2), COL_VS + g * HD, COL_VW + g * HD), g)
                tile_dma(N_GRP + 3, cols(w_in, slot(N_GRP + 3), g * R * HD + P), g)
            with sp.Fori(0, KT // RING) as i:
                for j in range(RING):
                    tile_dma(N_OUT + j, rows(w_out, slot(N_OUT + j), i * (RING * P) + j * P), i)
            with sp.Fori(0, FT // 2) as i:
                for j in range(RING):
                    tile_dma(N_UP + j, cols(w_up, slot(N_UP + j), i * (2 * P) + (j // 2) * P + (j % 2) * FF), i)
            for k in range(2):
                tile_dma(N_DOWN + k, rows(w_down, slot(N_DOWN + k), k * P))
            with sp.Fori(0, (FT - 2) // RING) as i:
                for j in range(RING):
                    tile_dma(N_DOWN + 2 + j, rows(w_down, slot(N_DOWN + 2 + j), i * (RING * P) + (2 + j) * P), i)
            for t in range(TB):
                sp.wait_ge(out_done, t + 1)
                sp.dma_start(out[0, t * P:(t + 1) * P, :], xs[:, t, :]).then_inc(stored, 16)
            sp.wait_ge(stored, 16 * TB)

        @block.gpsimd
        def _(pool):
            g = nc.gpsimd
            step = [0]

            def then(ins, wait=True):
                step[0] += 1
                ins.then_inc(const_ready, 1)
                if wait:
                    pool.wait_ge(const_ready, step[0])

            g.memset(stage[:, :, :], 0.0).then_inc(stage_clear, 1)
            then(g.memset(half_pow[:, :], -0.5), False)
            then(g.memset(ident[:, :], 0.0))
            then(g.affine_select(out=ident[:, :], in_=ident[:, :], compare_op=ALU.not_equal, fill=1.0, base=0,
                                 pattern=[[-1, P]], channel_multiplier=1))
            then(g.memset(valid[:, :], 1.0))
            then(g.affine_select(out=valid[:, :], in_=valid[:, :], compare_op=ALU.is_ge, fill=0.0, base=-(CMP - 1),
                                 pattern=[[0, 1]], channel_multiplier=1))
            dist, dist_c = bias[:, R - 1, :], bias_c[:, R - 1, :, :]
            then(g.iota(dist, pattern=[[-1, T]], base=T - P, channel_multiplier=1, allow_small_or_imprecise_dtypes=True))
            then(g.affine_select(out=dist, in_=dist, compare_op=ALU.is_ge, fill=MASKED, base=T - P,
                                 pattern=[[-1, T]], channel_multiplier=1))
            then(g.iota(dist_c, pattern=[[P, TB], [-STRIDE, NC]], base=-(CMP - 1), channel_multiplier=1,
                        allow_small_or_imprecise_dtypes=True))
            then(g.affine_select(out=dist_c, in_=dist_c, compare_op=ALU.is_ge, fill=MASKED, base=-(CMP - 1),
                                 pattern=[[P, TB], [-STRIDE, NC]], channel_multiplier=1))

            for z in (kc2, vc2):
                then(g.memset(z[:, :, T - 1:TP], 0.0))
            assert step[0] == N_CONST

            def rms(which):
                for t in range(TB):
                    pool.wait_ge(sq_done, TB * which + t + 1)
                    g.tensor_scalar(meansq[:, which, t:t + 1], sumsq[:, which, t:t + 1], 1.0 / D, EPS, ALU.mult, ALU.add)\
                        .then_inc(const_ready, 1)
                    step[0] += 1
                    pool.wait_ge(const_ready, step[0])
                    g.tensor_tensor(rstd[:, which, t:t + 1], meansq[:, which, t:t + 1], half_pow[:, t:t + 1], ALU.pow)\
                        .then_inc(rstd_done, 1)

            def low(n, more=None):
                s = slot(n)
                pool.wait_ge(wh_done, n + 1 if more is None else n + 1 + RING * more)
                g.tensor_tensor(wl[:, s, :], raw[:, s, :], wh[:, s, :].bitcast(F32), ALU.subtract).then_inc(wl_done, 1)

            def scale(X, par, b):
                pool.wait_ge(rs_done, 3 * X + 1 + b)
                pool.sem_inc(scale_begun, 1)
                for i in range(TB):
                    p = prob[:, par, b, poff(i):poff(i) + (i + 1) * P]
                    g.tensor_scalar(p, p, rs[:, par, 1 + b, i:i + 1], 1.0, ALU.mult, ALU.mult).then_inc(p_scaled, 1)

            def scale_head(X, par):
                scale(X, par, 0)
                scale(X, par, 1)

            low(N_GATE)
            rms(0)
            for n in range(N_CMP, N_GRP + 2 * RING):
                low(n)
            scale_head(0, 0)
            with pool.Fori(0, GROUPS - 1) as i:
                for r in range(R):
                    scale_head(R * i + r + 1, (r + 1) % 2)
                    low(N_GRP + 2 * RING + r, i)
            for r in range(R - 1):
                scale_head(R * (GROUPS - 1) + r + 1, (r + 1) % 2)
            for n in range(N_OUT + RING, N_UP + RING):
                low(n)
            rms(1)
            with pool.Fori(0, (N_DOWN + FT - 2 - N_UP - RING) // RING) as i:
                for j in range(RING):
                    low(N_UP + RING + j, i)
            for n in range(N_END - 2, N_END):
                low(n)
            rms(2)

        @block.scalar
        def _(act_):
            a = nc.scalar

            def high(n, more=None):
                s = slot(n)
                stream_wait(act_, n, more)
                if n >= RING:
                    act_.wait_ge(tile_done, n - RING + 1 if more is None else n - RING + 1 + RING * more)
                a.activation(wh[:, s, :], raw[:, s, :], ACT.Copy).then_inc(wh_done, 1)

            act_.wait_ge(stage_clear, 1)
            row = 0
            for src, n in ((attn_norm.rearrange("a (k p) -> (a k) p", p=P), KT), (mlp_norm.rearrange("a (k p) -> (a k) p", p=P), KT),
                           (cmp_pos[0].rearrange("c (j a) d -> (c j) (a d)", a=2), 2 * CJ),
                           (conv_b.rearrange("a (m p) -> (a m) p", p=P), 2 * FT)):
                a.dma_start(stage[row:row + n, 0, :], src).then_inc(vec_in, 16)
                row += n
            taps = conv_w[0].rearrange("i (m p) -> (i m) p", p=P)
            a.dma_start(stage[0:P, 1, :], taps[0:P]).then_inc(vec_in, 16)
            a.dma_start(stage[0:3 * 2 * FT - P, 2, :], taps[P:3 * 2 * FT]).then_inc(vec_in, 16)
            for e in range(2):
                a.dma_start(w2d[:, :, e, :], cmp_w2[0, 0].rearrange("(h p) d -> p h d", p=P)).then_inc(w2_in, 16)
            a.dma_start(w2v[:, :, :], cmp_w2[0, 1].rearrange("(h p) d -> p h d", p=P)).then_inc(w2_in, 16)
            a.dma_start(w1raw[:, :, :], cmp_w1[0, 0].rearrange("(j p) c -> p j c", p=P)).then_inc(w1_in[0], 16)

            def squares(which, src, ready):
                for t in range(TB):
                    ready(t)
                    a.activation(junk[:, t, :], src[:, t, :], ACT.Square, accum_out=sumsq[:, which, t:t + 1]).then_inc(sq_done, 1)

            junk = xn
            squares(0, xs, lambda t: act_.wait_ge(x_in[t], 16))
            high(N_GATE)

            def hT_high(which, gain):
                for k in range(KT):
                    act_.wait_ge(xT_ready, KT * which + k + 1)
                    a.activation(hT_h[:, k, :], bank[k % 4][:, :], ACT.Copy, scale=vec[:, gain + k:gain + k + 1]).then_inc(hT_h_done, 1)

            act_.wait_ge(vec_done, 3)
            hT_high(0, V_ANORM)
            high(N_CMP)
            high(N_CMP + 1)
            act_.wait_ge(tile_done, N_GATE + 1)
            a.activation(glT[:, :], pj[0][:, :], ACT.Copy).then_inc(glT_done, 1)
            act_.wait_ge(gateT_ready, 1)
            a.activation(gates[:, :, :, :],
                         pj[1][:, :].rearrange("p (i c) -> p i c", c=P)[:, :, GATE_ROW:P].rearrange("p i (h c) -> p h c i", c=3),
                         ACT.Tanh, scale=0.5).then_inc(gate_tanh, 1)
            high(N_CMP + 2)
            high(N_CMP + 3)

            def w1_high(c):
                act_.wait_ge(w1_in[c], 16)
                if c:
                    act_.wait_ge(hid_ready, 1)
                a.activation(w1h[:, :, :], w1raw[:, :, :], ACT.Copy).then_inc(w1h_done, 1)

            w1_high(0)
            act_.wait_ge(const_ready, N_CONST)
            for g in range(GROUPS):
                act_.wait_ge(tile_done, N_CMP + g + 1)
                src = pj[g % 2]
                a.activation(vc2[0:HD, g, 0:T], src[HD:P, :], ACT.Copy).then_inc(c_copied, 1)
                a.activation(vc2[HD:P, g, 0:T - 1], src[HD:P, 1:T], ACT.Copy).then_inc(c_copied, 1)
                high(N_GRP + g)

            for c in range(2):
                if c:
                    w1_high(1)
                act_.wait_ge(gel_step, 4 * c + 3)
                a.activation(gel2[0:GROUPS * NC, :], gel2[0:GROUPS * NC, :], ACT.Tanh, scale=GELU_C).then_inc(gel_tanh, 1)
                if c == 0:
                    act_.wait_ge(w1l_done, 1)
                    a.dma_start(w1raw[:, :, :], cmp_w1[0, 1].rearrange("(j p) c -> p j c", p=P)).then_inc(w1_in[1], 16)
                    act_.wait_ge(cmp_ready, 1)
                    a.activation(kkc_h[:, :, :].rearrange("p g n -> p (g n)"), sc[1][:, 0:GROUPS * NC], ACT.Copy).then_inc(kkch_done, 1)

            def exp_unit(G, w):
                r, u = divmod(w, UNITS)
                par = r % 2
                if u == UNITS - 1:
                    act_.wait_ge(c_shifted, R * G + r + 1)
                    a.activation(sc_c[:, par, :, :], sc_c[:, par, :, :], ACT.Exp, scale=-1.0).then_inc(c_exp, 1)
                    return
                b, i = divmod(u, TB)
                act_.wait_ge(masked, STEPS * G + w + 1 + C_MASKED)
                p = prob[:, par, b, poff(i):poff(i) + (i + 1) * P]
                a.activation(p, p, ACT.Exp, scale=-1.0, bias=mn[:, par, u:u + 1],
                             accum_out=sums[:, par, 1 + b, i:i + 1]).then_inc(exp_done, 1)

            def pt_high(G, w):
                n = unit_cols(w)
                act_.wait_ge(tr_ready, STEPS * G + w + 1 + C_TR)
                act_.wait_ge(av_done, STEPS * G + w + 1)
                a.activation(pt_h[:, w % PT_RING, 0:n], tr[w % TR_RING][:, 0:n], ACT.Copy).then_inc(pth_done, 1)

            def o_copy(G, r):
                half = (r % 2) * HD
                act_.wait_ge(av_done, STEPS * G + UNITS * (r + 1) + C_AV)
                a.activation(otmp[half:half + HD, :], ob[HD:P, :], ACT.Copy).then_inc(o_copied, 1)

            def o_high(G, r):
                half = (r % 2) * HD
                act_.wait_ge(o_summed, R * G + r + 1 + C_O)
                a.activation(oT_h[half:half + HD, bass.ds(2 * G + r // 2, 1), :], osum[half:half + HD, r % 2:r % 2 + 1, :], ACT.Copy)\
                    .then_inc(oh_done, 1)

            def q_high(G, q):
                act_.wait_ge(tile_done, RING * G + N_GRP + (4 if q else 1))
                for e in range(2):
                    rows_ = slice(HD * e, HD * e + HD)
                    a.activation(qq[rows_, 2 * q + e, :], pj[0][rows_, :], ACT.Copy, scale=-SCALE).then_inc(qh_done, 1)

            def k_high(G, b):
                act_.wait_ge(tile_done, RING * G + N_GRP + 2)
                for half in (b, 1 - b):
                    a.activation(kk_h[HD * half:HD * half + HD, b, :], pj[1][HD * b:HD * b + HD, :], ACT.Copy).then_inc(kvh_done, 1)

            def v_copy(G):
                act_.wait_ge(tile_done, RING * G + N_GRP + 3)
                a.activation(vT[:, :], pj[0][:, :], ACT.Copy).then_inc(vT_done, 1)

            def v_high(G):
                act_.wait_ge(gateT_ready, G + 2)
                a.activation(vv[:, :, :, 0, :], pj[1][:, :].rearrange("p (t b d) -> p b t d", t=TB, b=2), ACT.Copy).then_inc(kvh_done, 1)

            def steps(G, first, last, project_next):
                for w in range(first, last):
                    r, u = divmod(w, UNITS)
                    if w >= 0 and r and u == BEHIND:
                        o_copy(G, r - 1)
                    if w >= 0 and r and u == BEHIND + 1:
                        o_high(G, r - 1)
                    if w >= 0:
                        pt_high(G, w)
                    if (project_next or w + AHEAD - 1 < STEPS) and w + AHEAD - 1 >= 0:
                        exp_unit(G, w + AHEAD - 1)
                    if not project_next:
                        continue
                    if w == 7:
                        act_.wait_ge(scores_ready, STEPS * G + 2 * UNITS)
                        q_high(G + 1, 0)
                        high(N_GRP + 2 * RING + 0, G)
                    if w == 17:
                        act_.wait_ge(scores_ready, STEPS * G + 3 * UNITS + TB)
                        k_high(G + 1, 0)
                        high(N_GRP + 2 * RING + 1, G)
                    if w == 19:
                        v_copy(G + 1)
                    if w == 21:
                        act_.wait_ge(scores_ready, STEPS * G + 3 * UNITS + 2 * TB)
                        k_high(G + 1, 1)
                        high(N_GRP + 2 * RING + 2, G)
                    if w == 27:
                        act_.wait_ge(scores_ready, STEPS * G + 4 * UNITS)
                        q_high(G + 1, 1)
                    if w == 29:
                        high(N_GRP + 2 * RING + 3, G)

            q_high(0, 0)
            high(N_GRP + RING)
            k_high(0, 0)
            k_high(0, 1)
            high(N_GRP + RING + 1)
            v_copy(0)
            high(N_GRP + RING + 2)
            q_high(0, 1)
            high(N_GRP + RING + 3)
            v_high(0)
            steps(0, -AHEAD, 0, True)
            with act_.Fori(0, GROUPS - 1) as G:
                steps(G, 0, STEPS, True)
                o_copy(G, R - 1)
                act_.wait_ge(av_done, STEPS * G + STEPS + C_AV)
                v_high(G + 1)
                o_high(G, R - 1)
            steps(GROUPS - 1, 0, STEPS, False)
            o_copy(GROUPS - 1, R - 1)
            o_high(GROUPS - 1, R - 1)
            for n in range(N_OUT + RING, N_UP + RING):
                high(n)
            for t in range(TB):
                act_.wait_ge(x1_done, 2 * t + 2)
                a.activation(x1n[:, t, :], xs[:, t, :], ACT.Square, accum_out=sumsq[:, 1, t:t + 1]).then_inc(sq_done, 1)
            hT_high(1, V_MNORM)

            with act_.Fori(0, FT // 2) as i:
                for m in range(2):
                    for h in range(2):
                        j = 2 * m + h
                        act_.wait_ge(tile_done, 4 * i + N_UP + j + 1)
                        act_.wait_ge(act_done, 2 * i + m + 1)
                        col = 2 * i + (m + h * FT)
                        a.activation(conv[:, j, :], bank[j][:, :], ACT.Identity,
                                     scale=vec[:, bass.ds(col + (V_CW + 2 * 2 * FT), 1)], bias=vec[:, bass.ds(col + V_CB, 1)])\
                            .then_inc(conv0, 1)
                        high(N_UP + RING + j, i)
                    act_.wait_ge(conv_done, 4 * i + 2 * m + 2 + C_CONV)
                    a.activation(th[:, m, :], conv[:, 2 * m + 1, :], ACT.Tanh, scale=0.5).then_inc(g_tanh, 1)
                    act_.wait_ge(act_done, 2 * i + m + 1 + C_AH)
                    a.activation(aT_h[:, bass.ds(2 * i + m, 1), :], act[:, m:m + 1, :], ACT.Copy).then_inc(ah_done, 1)
            for n in range(N_DOWN + RING, N_DOWN + 2 + RING):
                high(n)
            with act_.Fori(0, (FT - 2 - RING) // RING) as i:
                for j in range(RING):
                    high(N_DOWN + 2 + RING + j, i)
            a.dma_start(fgain[:, :], final_norm.rearrange("(a d) -> a d", a=1).broadcast_to([P, D])).then_inc(fgain_in, 16)
            for n in range(0, KT, 2):
                act_.wait_ge(yT_ready, n + 1)
                a.activation(yT[:, n, :], bank[n][:, :], ACT.Copy).then_inc(yT_act, 1)
            for t in range(TB):
                act_.wait_ge(x2_done, 2 * t + 2)
                a.activation(raw[:, t, :], xs[:, t, :], ACT.Square, accum_out=sumsq[:, 2, t:t + 1]).then_inc(sq_done, 1)

        @block.vector
        def _(dve):
            v_ = nc.vector
            dve.sem_inc(masked, C_MASKED)
            dve.sem_inc(pt_done, C_PT)
            dve.sem_inc(o_summed, C_O)
            dve.sem_inc(conv_done, C_CONV)
            dve.sem_inc(act_done, C_AH)

            def normed(which, dst):
                for t in range(TB):
                    dve.wait_ge(rstd_done, TB * which + t + 1)
                    v_.tensor_scalar(dst[:, t, :], xs[:, t, :], rstd[:, which, t:t + 1], None, ALU.mult).then_inc(xn_done, 1)

            def hT_low(which, gain):
                for k in range(KT):
                    dve.wait_ge(hT_h_done, KT * which + k + 1)
                    v_.scalar_tensor_tensor(hT_l[:, k, :], bank[k % 4][:, :], vec[:, gain + k:gain + k + 1],
                                            hT_h[:, k, :].bitcast(F32), ALU.mult, ALU.subtract).then_inc(hT_done, 1)

            for n, (c0, c1) in enumerate(((0, V_A), (V_A, V_A + P), (V_A + P, V_CW + 3 * 2 * FT))):
                dve.wait_ge(vecT_ready, n + 1)
                v_.tensor_copy(vec[:, c0:c1], bank[4 + n][:, 0:c1 - c0]).then_inc(vec_done, 1)
            dve.wait_ge(const_ready, N_CONST)
            for r in range(R):
                s = slopes()[r]
                if r == R - 1:
                    dve.wait_ge(bias_done, 2 * r)
                v_.tensor_scalar(bias[:, r, :], bias[:, R - 1, :], s, None, ALU.mult).then_inc(bias_done, 1)
                v_.tensor_scalar(bias_c[:, r, :, :], bias_c[:, R - 1, :, :], s, None, ALU.mult).then_inc(bias_done, 1)
            normed(0, xn)
            dve.wait_ge(vec_done, 3)
            hT_low(0, V_ANORM)
            dve.wait_ge(gate_tanh, 1)
            v_.tensor_scalar(gates[:, :, :, :], gates[:, :, :, :], 0.5, 0.5, ALU.mult, ALU.add).then_inc(gates_done, 1)
            dve.wait_ge(gates_done, 1)
            v_.tensor_scalar(gates[:, :, 0, 0], gates[:, :, 0, 0], valid[:, 0:1], None, ALU.mult).then_inc(gates_done, 1)

            def w1_low(c):
                dve.wait_ge(w1h_done, c + 1)
                v_.tensor_tensor(w1l[:, :, :], w1raw[:, :, :], w1h[:, :, :].bitcast(F32), ALU.subtract).then_inc(w1l_done, 1)

            w1_low(0)
            for g in range(GROUPS):
                dve.wait_ge(tile_done, N_CMP + g + 1)
                src = pj[g % 2]
                v_.tensor_copy(kc2[0:HD, g, 0:T], src[0:HD, :])
                v_.tensor_copy(kc2[HD:P, g, 0:T - 1], src[0:HD, 1:T]).then_inc(pj_evac, 1)

            nb = GROUPS * NC
            for c, src in enumerate((kc2, vc2)):
                if c:
                    w1_low(1)
                    dve.wait_ge(hid_ready, 1)
                    dve.wait_ge(c_copied, 2 * GROUPS)
                else:
                    dve.wait_ge(pj_evac, GROUPS)
                for j in range(CJ):
                    window = src[:, :, 2 * j:2 * j + STRIDE * (NC - 1) + 1:STRIDE]
                    pos = vec[:, V_POS + c * CJ + j:V_POS + c * CJ + j + 1]
                    v_.tensor_scalar(blk_h[:, j, :, :], window, pos, None, ALU.add).then_inc(blkh_done, 1)
                    dve.wait_ge(blkh_done, c * CJ + j + 1)
                    v_.scalar_tensor_tensor(blk_l[:, j, :, :], window, pos, blk_h[:, j, :, :].bitcast(F32), ALU.add, ALU.subtract)\
                        .then_inc(blk_done, 1)
                hid = sc[0][0:nb, 0:HID]
                dve.wait_ge(hid_ready, c + 1)
                v_.tensor_copy(gel[0:nb, :], hid).then_inc(gel_step, 1)
                dve.wait_ge(gel_step, 4 * c + 1)
                v_.tensor_tensor(gel2[0:nb, :], gel[0:nb, :], gel[0:nb, :], ALU.mult).then_inc(gel_step, 1)
                dve.wait_ge(gel_step, 4 * c + 2)
                v_.tensor_scalar(gel2[0:nb, :], gel2[0:nb, :], 0.044715, 1.0, ALU.mult, ALU.add).then_inc(gel_mid, 1)
                dve.wait_ge(gel_mid, 2 * c + 1)
                v_.tensor_tensor(gel2[0:nb, :], gel2[0:nb, :], gel[0:nb, :], ALU.mult).then_inc(gel_step, 1)
                dve.wait_ge(gel_tanh, c + 1)
                v_.tensor_scalar(gel2[0:nb, :], gel2[0:nb, :], 0.5, 0.5, ALU.mult, ALU.add).then_inc(gel_mid, 1)
                dve.wait_ge(gel_mid, 2 * c + 2)
                v_.tensor_tensor(gel[0:nb, :], gel2[0:nb, :], gel[0:nb, :], ALU.mult).then_inc(gel_step, 1)
                dve.wait_ge(gelT_ready, c + 1)
                if c == 0:
                    v_.tensor_copy(gT[:, :, :], cc[:, 0:2 * nb].rearrange("p (a n) -> p a n", a=2)).then_inc(gT_done, 1)
                    dve.wait_ge(kkch_done, 1)
                    v_.tensor_tensor(kkc_l[:, :, :].rearrange("p g n -> p (g n)"), sc[1][:, 0:nb],
                                     kkc_h[:, :, :].rearrange("p g n -> p (g n)").bitcast(F32), ALU.subtract).then_inc(cmp_done, 1)
                else:
                    for rep in range(TB):
                        v_.tensor_copy(gTr[:, :, :, rep, :], cc[:, 0:2 * nb].rearrange("p (a g n) -> p g a n", a=2, g=GROUPS)).then_inc(gT_done, 1)
                    dve.wait_ge(cmp_ready, 2)
                    v_.tensor_copy(vvc_all[:, :, :], sc[1][:, 0:GROUPS * HD].rearrange("p (g d) -> p g d", g=GROUPS)).then_inc(cmp_done, 1)
            v_.memset(pbd[:, :, :, :, :].rearrange("p a b c n -> p (a b c n)"), 0.0).then_inc(gel_mid, 1)
            dve.wait_ge(gel_mid, 5)

            def mask_unit(G, w):
                r, u = divmod(w, UNITS)
                par, head = r % 2, r % R
                b, i = divmod(u, TB)
                n = (i + 1) * P
                dve.wait_ge(scores_ready, STEPS * G + w + 1)
                if u == UNITS - 1:
                    s = sc_c[:, par, :, :]
                    v_.tensor_tensor(s, sc[w % SC_RING][:, 0:TB * NC].rearrange("p (i n) -> p i n", i=TB), bias_c[:, head, :, :], ALU.add)\
                        .then_inc(masked, 1)
                    dve.wait_ge(masked, STEPS * G + w + 1 + C_MASKED)
                    v_.tensor_reduce(mn_c[:, par, :], s, AX, ALU.min).then_inc(c_min, 1)
                    v_.tensor_scalar(bias[:, head, :], bias[:, head, :], SLOPE_STEP, None, ALU.mult).then_inc(bias_done, 1)
                    v_.tensor_scalar(bias_c[:, head, :, :], bias_c[:, head, :, :], SLOPE_STEP, None, ALU.mult).then_inc(bias_done, 1)
                    dve.wait_ge(c_min, R * G + r + 1)
                    v_.tensor_tensor(s, s, mn_c[:, par, :].unsqueeze(2).broadcast_to([P, TB, NC]), ALU.subtract).then_inc(c_shifted, 1)
                    return
                if i == 0:
                    dve.wait_ge(tr_ready, STEPS * G + UNITS * (r - 2) + (1 + b) * TB + C_TR)
                dve.sem_inc(mask_begun, 1)
                v_.tensor_tensor_reduce(prob[:, par, b, poff(i):poff(i) + n], sc[w % SC_RING][:, 0:n], bias[:, head, T - n:T], 1.0, MASKED * 10,
                                        ALU.add, ALU.min, mn[:, par, u:u + 1]).then_inc(masked, 1)

            def row_scales(G, r, c):
                par = r % 2
                X, k = R * G + r, {1: 1, 2: 2, 0: 3}[c]
                if c == 0:
                    dve.wait_ge(c_exp, X + 1)
                    v_.tensor_reduce(sums[:, par, 0, :], sc_c[:, par, :, :], AX, ALU.add).then_inc(c_sum, 1)
                    dve.wait_ge(c_sum, X + 1)
                else:
                    dve.wait_ge(exp_done, 2 * TB * X + TB * c)
                v_.reciprocal(rs[:, par, c, :], sums[:, par, c, :]).then_inc(recip_done, 1)
                dve.wait_ge(recip_done, 3 * X + k)
                v_.tensor_tensor(rs[:, par, c:c + 1, :], rs[:, par, c:c + 1, :], gates[:, bass.ds(X, 1), c, :], ALU.mult).then_inc(rs_done, 1)

            def diagonal(G, r):
                par = r % 2
                X = R * G + r
                dve.wait_ge(rs_done, 3 * X + 3)
                dve.wait_ge(tr_ready, STEPS * G + UNITS * (r - 1) + C_TR)
                diag = pbd[:, par, :, :, :].rearrange("p i j n -> p (i j) n")[:, 0:TB * TB:TB + 1, :]
                v_.tensor_tensor(diag, sc_c[:, par, :, :], rs[:, par, 0, :].unsqueeze(2).broadcast_to([P, TB, NC]), ALU.mult).then_inc(diag_done, 1)

            def pt_low(G, w):
                n = unit_cols(w)
                dve.wait_ge(pth_done, STEPS * G + w + 1)
                s = w % PT_RING
                v_.tensor_tensor(pt_l[:, s, 0:n], tr[w % TR_RING][:, 0:n], pt_h[:, s, 0:n].bitcast(F32), ALU.subtract).then_inc(pt_done, 1)

            def o_sum(G, r):
                half = (r % 2) * HD
                dve.wait_ge(o_copied, R * G + r + 1)
                v_.tensor_tensor(osum[half:half + HD, r % 2, :], ob[0:HD, :], otmp[half:half + HD, :], ALU.add).then_inc(o_summed, 1)

            def o_low(G, r):
                half = (r % 2) * HD
                dve.wait_ge(oh_done, R * G + r + 1)
                dst = (slice(half, half + HD), bass.ds(2 * G + r // 2, 1), slice(None))
                v_.tensor_tensor(oT_l[dst], osum[half:half + HD, r % 2:r % 2 + 1, :], oT_h[dst].bitcast(F32), ALU.subtract).then_inc(oT_done, 1)

            def q_low(G, q):
                for e in range(2):
                    rows_, other = slice(HD * e, HD * e + HD), slice(HD - HD * e, P - HD * e)
                    dve.wait_ge(qh_done, 4 * G + 2 * q + e + 1)
                    m = v_.scalar_tensor_tensor(qq[other, 2 * q + e, :], pj[0][rows_, :], -SCALE, qq[rows_, 2 * q + e, :].bitcast(F32),
                                                ALU.mult, ALU.subtract)
                m.then_inc(pj_evac, 1)

            def k_low(G, b):
                same, other = slice(HD * b, HD * b + HD), slice(HD - HD * b, P - HD * b)
                dve.wait_ge(kvh_done, 5 * G + 2 * b + 2)
                for dst in (same, other):
                    m = v_.tensor_tensor(kk_l[dst, b, :], pj[1][same, :], kk_h[same, b, :].bitcast(F32), ALU.subtract)
                m.then_inc(pj_evac, 1)

            def v_low(G):
                dve.wait_ge(kvh_done, 5 * G + 5)
                v_.tensor_tensor(vv[:, :, :, 1, :], pj[1][:, :].rearrange("p (t b d) -> p b t d", t=TB, b=2), vv[:, :, :, 0, :].bitcast(F32),
                                 ALU.subtract).then_inc(pj_evac, 1)
                v_.tensor_copy(vvc[:, 0:1, :], vvc_all[:, bass.ds(G, 1), :]).then_inc(vvc_done, 1)
                dve.wait_ge(vvc_done, 2 * G + 1)
                v_.tensor_tensor(vvc[:, 1:2, :], vvc_all[:, bass.ds(G, 1), :], vvc[:, 0:1, :].bitcast(F32), ALU.subtract).then_inc(vvc_done, 1)

            def steps(G, first, last, project_next):
                for w in range(first, last):
                    r, u = divmod(w, UNITS)
                    if w >= 0 and r and u == BEHIND:
                        o_sum(G, r - 1)
                    if w >= 0 and r and u == BEHIND + 1:
                        o_low(G, r - 1)
                    if project_next or w + AHEAD < STEPS:
                        mask_unit(G, w + AHEAD)
                    if w >= 0:
                        pt_low(G, w)
                    for before, what in ((8, 1), (4, 2), (3, 0), (2, None)):
                        X, rest = divmod(w + before, UNITS)
                        if rest == 0 and X >= 0 and (project_next or X < R):
                            row_scales(G, X, what) if what is not None else diagonal(G, X)
                    if project_next and w == 7:
                        q_low(G + 1, 0)
                    if project_next and w == 17:
                        k_low(G + 1, 0)
                    if project_next and w == 21:
                        k_low(G + 1, 1)
                    if project_next and w == 27:
                        q_low(G + 1, 1)

            dve.wait_ge(cmp_done, 2)
            q_low(0, 0)
            k_low(0, 0)
            k_low(0, 1)
            q_low(0, 1)
            v_low(0)
            dve.wait_ge(bias_done, 2 * R)
            steps(0, -AHEAD, 0, True)
            with dve.Fori(0, GROUPS - 1) as G:
                dve.wait_ge(bias_done, 2 * R * G + 2 * R + 2)
                steps(G, 0, STEPS, True)
                o_sum(G, R - 1)
                v_low(G + 1)
                o_low(G, R - 1)
            steps(GROUPS - 1, 0, STEPS, False)
            o_sum(GROUPS - 1, R - 1)
            o_low(GROUPS - 1, R - 1)

            for t in range(TB):
                for h in range(2):
                    if 2 * t + h < 2 * TB - 1:
                        dve.wait_ge(y_ready, 2 * t + h + 1)
                    else:
                        dve.wait_ge(tile_done, N_UP)
                    cols_ = slice(512 * h, 512 * h + 512)
                    v_.tensor_tensor(xs[:, t, cols_], bank[2 * t + h][:, :], xs[:, t, cols_], ALU.add).then_inc(x1_done, 1)
            normed(1, x1n)
            hT_low(1, V_MNORM)

            with dve.Fori(0, FT // 2) as i:
                for m in range(2):
                    for h in range(2):
                        j = 2 * m + h
                        for tap, back in ((1, 1), (0, 2)):
                            dve.wait_ge(conv0 if tap else conv1, 4 * i + j + 1)
                            col = 2 * i + (m + h * FT + V_CW + tap * 2 * FT)
                            v_.scalar_tensor_tensor(conv[:, j, back:T], bank[j][:, 0:T - back], vec[:, bass.ds(col, 1)], conv[:, j, back:T],
                                                    ALU.mult, ALU.add).then_inc(conv1 if tap else conv_done, 1)
                    dve.wait_ge(g_tanh, 2 * i + m + 1)
                    v_.scalar_tensor_tensor(th[:, m, :], th[:, m, :], 1.0, conv[:, 2 * m + 1, :], ALU.add, ALU.mult).then_inc(silu_done, 1)
                    dve.wait_ge(silu_done, 2 * i + m + 1)
                    v_.scalar_tensor_tensor(act[:, m, :], th[:, m, :], 0.5, conv[:, 2 * m, :], ALU.mult, ALU.mult).then_inc(act_done, 1)
                    dve.wait_ge(ah_done, 2 * i + m + 1)
                    v_.tensor_tensor(aT_l[:, bass.ds(2 * i + m, 1), :], act[:, m:m + 1, :], aT_h[:, bass.ds(2 * i + m, 1), :].bitcast(F32),
                                     ALU.subtract).then_inc(aT_done, 1)
            for n in range(1, KT, 2):
                dve.wait_ge(yT_ready, n + 1)
                v_.tensor_copy(yT[:, n, :], bank[n][:, :]).then_inc(yT_dve, 1)
            for t in range(TB):
                for h in range(2):
                    dve.wait_ge(z_ready, 2 * t + h + 1)
                    cols_ = slice(512 * h, 512 * h + 512)
                    v_.tensor_tensor(xs[:, t, cols_], bank[2 * t + h][:, :], xs[:, t, cols_], ALU.add).then_inc(x2_done, 1)
            dve.wait_ge(fgain_in, 16)
            for t in range(TB):
                dve.wait_ge(rstd_done, 2 * TB + t + 1)
                v_.scalar_tensor_tensor(xs[:, t, :], xs[:, t, :], rstd[:, 2, t:t + 1], fgain[:, :], ALU.mult, ALU.mult).then_inc(out_done, 1)

        @block.tensor
        def _(pe):
            t_ = nc.tensor
            pe.sem_inc(tr_ready, C_TR)
            pe.sem_inc(av_done, C_AV)

            def xT(which, src, gain):
                for k in range(KT):
                    if k == 0:
                        pe.wait_ge(xn_done, TB * which + TB)
                    if k >= 4:
                        pe.wait_ge(hT_done, KT * which + k - 3)
                    for t in range(TB):
                        m = t_.transpose(bank[k % 4][:, t * P:(t + 1) * P], src[:, t, k * P:(k + 1) * P], ident[:, :])
                    m.then_inc(xT_ready, 1)

            def tile_ready(n, more=None):
                pe.wait_ge(wl_done, n + 1 if more is None else n + 1 + RING * more)

            def project(n, dst, more=None, k0=0, k1=KT):
                if k0 == 0:
                    tile_ready(n, more)
                s = slot(n)
                for k in range(k0, k1):
                    c = slice(k * P, (k + 1) * P)
                    t_.matmul(dst[:, :], wh[:, s, c], hT_h[:, k, :], start=(k == 0), stop=False)
                    t_.matmul(dst[:, :], wh[:, s, c], hT_l[:, k, :], start=False, stop=False)
                    m = t_.matmul(dst[:, :], wl[:, s, c], hT_h[:, k, :], start=False, stop=(k == KT - 1))
                if k1 == KT:
                    m.then_inc(tile_done, 1)

            pe.wait_ge(vec_in, 16 * 6)
            pe.wait_ge(const_ready, 3)
            for n in range(3):
                t_.transpose(bank[4 + n][:, 0:P], stage[:, n, :], ident[:, :]).then_inc(vecT_ready, 1)
            xT(0, xn, V_ANORM)
            pe.wait_ge(hT_done, KT)
            project(N_GATE, pj[0])
            pe.wait_ge(glT_done, 1)
            for t in range(TB):
                m = t_.transpose(pj[1][:, t * P:(t + 1) * P], glT[:, t * P:(t + 1) * P], ident[:, :])
            m.then_inc(gateT_ready, 1)
            for g in range(GROUPS):
                if g == 1:
                    pe.wait_ge(gate_tanh, 1)
                if g >= 2:
                    pe.wait_ge(pj_evac, g - 1)
                    pe.wait_ge(c_copied, 2 * (g - 1))
                project(N_CMP + g, pj[g % 2])

            nb = GROUPS * NC
            pe.wait_ge(w2_in, 48)
            for c in range(2):
                pe.wait_ge(w1l_done, c + 1)
                for j in range(CJ):
                    pe.wait_ge(blk_done, c * CJ + j + 1)
                    bh = blk_h[:, j, :, :].rearrange("p g n -> p (g n)")
                    bl = blk_l[:, j, :, :].rearrange("p g n -> p (g n)")
                    dst = sc[0][0:nb, 0:HID]
                    if c and j == 0:
                        pe.wait_ge(gel_step, 4)
                    t_.matmul(dst, bh, w1h[:, j, :], start=(j == 0), stop=False)
                    t_.matmul(dst, bh, w1l[:, j, :], start=False, stop=False)
                    m = t_.matmul(dst, bl, w1h[:, j, :], start=False, stop=(j == CJ - 1))
                m.then_inc(hid_ready, 1)
                pe.wait_ge(gel_step, 4 * c + 4)
                for h in range(2):
                    m = t_.transpose(cc[:, h * nb:h * nb + nb], gel[0:nb, h * P:(h + 1) * P], ident[0:nb, 0:nb])
                m.then_inc(gelT_ready, 1)
                pe.wait_ge(gT_done, TB * c + 1)
                if c == 0:
                    for h in range(2):
                        m = t_.matmul(sc[1][:, 0:nb], w2d[:, h, :, :].rearrange("p e d -> p (e d)"), gT[:, h, :], start=(h == 0), stop=(h == 1))
                    m.then_inc(cmp_ready, 1)
                else:
                    pe.wait_ge(cmp_done, 1)
                    for g in range(GROUPS):
                        for h in range(2):
                            m = t_.matmul(sc[1][0:nb, g * HD:(g + 1) * HD], gTr[:, g, h, :, :].rearrange("p r n -> p (r n)"), w2v[:, h, :], start=(h == 0), stop=(h == 1))
                    m.then_inc(cmp_ready, 1)

            def score_unit(G, w):
                r, u = divmod(w, UNITS)
                b, i = divmod(u, TB)
                dst = sc[w % SC_RING]
                pe.wait_ge(masked, STEPS * G + w + 1)
                if u < UNITS - 1:
                    n = (i + 1) * P
                    q = qq[:, r % R, i * P:(i + 1) * P]
                    t_.matmul(dst[:, 0:n], q, kk_h[:, b, 0:n], start=True, stop=False)
                    t_.matmul(dst[:, 0:n], q, kk_l[:, b, 0:n], start=False, stop=True).then_inc(scores_ready, 1)
                    return
                kh, kl = (z[:, bass.ds(G + r // R, 1), :].rearrange("p a n -> p (a n)") for z in (kkc_h, kkc_l))
                for i in range(TB):
                    q = qq[:, r % R, i * P:(i + 1) * P]
                    t_.matmul(dst[:, i * NC:(i + 1) * NC], q, kh, start=True, stop=False)
                    m = t_.matmul(dst[:, i * NC:(i + 1) * NC], q, kl, start=False, stop=True)
                m.then_inc(scores_ready, 1)

            def transpose_unit(G, w):
                r, u = divmod(w, UNITS)
                b, j = divmod(u, TB)
                X, par, dst = R * G + r, r % 2, tr[w % TR_RING]
                pe.wait_ge(pt_done, STEPS * G + w + 1)
                if u == UNITS - 1:
                    pe.wait_ge(diag_done, X + 1)
                    for i in range(TB):
                        m = t_.transpose(dst[:, i * P:(i + 1) * P], pbd[:, par, i, :, :].rearrange("p j n -> p (j n)"), ident[:, :])
                else:
                    if j == 0:
                        pe.wait_ge(p_scaled, 2 * TB * X + TB * (b + 1))
                    for i in range(j, TB):
                        m = t_.transpose(dst[:, (i - j) * P:(i - j + 1) * P], prob[:, par, b, poff(i) + j * P:poff(i) + (j + 1) * P], ident[:, :])
                m.then_inc(tr_ready, 1)

            def value_unit(G, w):
                r, u = divmod(w, UNITS)
                b, j = divmod(u, TB)
                s, n = w % PT_RING, unit_cols(w)
                if u == 0:
                    pe.wait_ge(o_summed, R * G + r + 1)
                pe.wait_ge(pt_done, STEPS * G + w + 1 + C_PT)
                w_ = (vvc[:, :, :] if u == UNITS - 1 else vv[:, b, j, :, :]).rearrange("p a d -> p (a d)")
                dst = ob[:, T - n:T]
                t_.matmul(dst, w_, pt_h[:, s, 0:n], start=(u == 0), stop=False)
                t_.matmul(dst, w_, pt_l[:, s, 0:n], start=False, stop=(u == UNITS - 1)).then_inc(av_done, 1)

            def evacuated(G, n):
                pe.wait_ge(pj_evac, 5 * G + n + GROUPS)

            def v_transpose(G):
                pe.wait_ge(vT_done, G + 1)
                evacuated(G, 3)
                for t in range(TB):
                    m = t_.transpose(pj[1][:, t * P:(t + 1) * P], vT[:, t * P:(t + 1) * P], ident[:, :])
                m.then_inc(gateT_ready, 1)

            def steps(G, first, last, project_next):
                for w in range(first, last):
                    if project_next or w + AHEAD < STEPS:
                        if w + AHEAD == STEPS:
                            evacuated(G + 1, 2)
                        if w + AHEAD == STEPS + TB:
                            evacuated(G + 1, 3)
                        score_unit(G, w + AHEAD)
                    if w < 0:
                        continue
                    transpose_unit(G, w)
                    if project_next:
                        if w == 12:
                            evacuated(G + 1, 1)
                        if w == 20:
                            pe.wait_ge(vT_done, G + 2)
                        for tile, at, dst in ((0, 0, pj[0]), (1, 6, pj[1]), (2, 12, pj[0]), (3, 20, pj[0])):
                            k0, k1 = (min(KT, max(0, (w + d - at) * KT // 6)) for d in (0, 1))
                            if k1 > k0:
                                project(N_GRP + RING + tile, dst, G, k0, k1)
                        if w == 28:
                            v_transpose(G + 1)
                    if w >= BEHIND:
                        value_unit(G, w - BEHIND)

            project(N_GRP, pj[0])
            project(N_GRP + 1, pj[1])
            evacuated(0, 1)
            project(N_GRP + 2, pj[0])
            v_transpose(0)
            project(N_GRP + 3, pj[0])
            evacuated(0, 4)
            steps(0, -AHEAD, 0, True)
            with pe.Fori(0, GROUPS - 1) as G:
                evacuated(G, 5)
                pe.wait_ge(vvc_done, 2 * G + 2)
                steps(G, 0, STEPS, True)
                for w in range(STEPS - BEHIND, STEPS):
                    value_unit(G, w)
            evacuated(GROUPS - 1, 5)
            pe.wait_ge(vvc_done, 2 * GROUPS)
            steps(GROUPS - 1, 0, STEPS, False)
            for w in range(STEPS - BEHIND, STEPS):
                value_unit(GROUPS - 1, w)

            pe.wait_ge(oT_done, HEADS)
            pe.wait_ge(masked, STEPS * GROUPS + C_MASKED)
            for k in range(KT):
                n = N_OUT + k
                tile_ready(n)
                s = slot(n)
                for t in range(TB):
                    tc = slice(t * P, (t + 1) * P)
                    for o, w in ((oT_h, wh), (oT_h, wl), (oT_l, wh)):
                        for h in range(2):
                            m = t_.matmul(bank[2 * t + h][:, :], o[:, k, tc], w[:, s, 512 * h:512 * h + 512],
                                          start=(k == 0 and o is oT_h and w is wh), stop=(k == KT - 1 and o is oT_l))
                            if k == KT - 1 and o is oT_l and 2 * t + h < 2 * TB - 1:
                                m.then_inc(y_ready, 1)
                m.then_inc(tile_done, 1)
            pe.wait_ge(x1_done, 2 * TB)
            xT(1, x1n, V_MNORM)
            pe.wait_ge(hT_done, 2 * KT)

            with pe.Fori(0, FT // 2) as i:
                for j in range(RING):
                    pe.wait_ge(conv_done, 4 * i + j + 1)
                    project(N_UP + j, bank[j], i)

            pe.wait_ge(conv_done, 2 * FT + C_CONV)

            def down(k, n, more=None, last=False):
                pe.wait_ge(aT_done, k + 1)
                tile_ready(n, more)
                s = slot(n)
                first = more is None and n == N_DOWN
                ah, al = aT_h[:, bass.ds(k, 1), :], aT_l[:, bass.ds(k, 1), :]
                ah, al = (z.rearrange("p a t -> p (a t)") for z in (ah, al))
                for c in range(KT):
                    cs = slice(c * P, (c + 1) * P)
                    t_.matmul(bank[c][:, :], wh[:, s, cs], ah, start=first, stop=False, skip_group_check=True)
                    t_.matmul(bank[c][:, :], wh[:, s, cs], al, start=False, stop=False, skip_group_check=True)
                    m = t_.matmul(bank[c][:, :], wl[:, s, cs], ah, start=False, stop=last, skip_group_check=True)
                    if last:
                        m.then_inc(yT_ready, 1)
                if not last:
                    m.then_inc(tile_done, 1)

            for k in range(2):
                down(k, N_DOWN + k)
            with pe.Fori(0, (FT - 2 - RING) // RING) as i:
                for j in range(RING):
                    down(i * RING + (2 + j), N_DOWN + 2 + j, i)
            for k in range(FT - RING, FT):
                down(k, N_DOWN + k, None, k == FT - 1)
            pe.wait_ge(yT_act, KT // 2)
            pe.wait_ge(yT_dve, KT // 2)
            for t in range(TB):
                for h in range(2):
                    for c in range(4):
                        m = t_.transpose(bank[2 * t + h][:, c * P:(c + 1) * P], yT[:, 4 * h + c, t * P:(t + 1) * P], ident[:, :])
                    m.then_inc(z_ready, 1)


_INS = ['x', 'attn_norm', 'mlp_norm', 'final_norm', 'nsa_w_in', 'nsa_cmp_pos', 'nsa_cmp_w1', 'nsa_cmp_w2', 'nsa_w_out',
        'mlp_w_up', 'mlp_conv_w', 'mlp_conv_b', 'mlp_w_down']


def kernel(**inputs):
    import numpy as _np
    import concourse.bacc as _bacc
    from concourse import mybir as _mybir
    from concourse.bass_utils import run_bass_kernel_spmd as _run

    nc = _bacc.Bacc("TRN2", target_bir_lowering=False, num_devices=1, dynamic_dma_scratch_size=1024)
    arrays, args = {}, []
    for name in _INS:
        a = _np.ascontiguousarray(inputs[name])
        arrays[f"in_{name}"] = a
        args.append(nc.dram_tensor(f"in_{name}", a.shape, _mybir.dt.from_np(a.dtype), kind="ExternalInput").ap())
    args.append(nc.dram_tensor("out_x", (1, T, D), F32, kind="ExternalOutput").ap())
    build(nc, *args)
    r = _run(nc, [arrays], core_ids=[0])
    return r.results[0]["out_x"]
```

```python
from contextlib import ExitStack

import concourse.bass as bass
from concourse import mybir

F32 = mybir.dt.float32
F32R = mybir.dt.float32r
ALU = mybir.AluOpType
ACT = mybir.ActivationFunctionType
AX = mybir.AxisListType.X

P = 128
T = 512
D = 1024
TB = T // P
KT = D // P
HD = 64
HEADS = D // HD
GROUPS = 4
R = HEADS // GROUPS
KV = GROUPS * HD
COL_KC, COL_VC, COL_KS, COL_VS, COL_KW, COL_VW, COL_GATE = (D + n * KV for n in range(7))
W_IN = COL_GATE + 3 * HEADS
COL_GATE_TILE = W_IN - P
GATE_ROW = P - 3 * HEADS
CMP, STRIDE = 32, 16
NC = T // STRIDE
TP = T + CMP // 2
CJ = CMP * HD // P
HID = 256
FF = 2816
FT = FF // P
EPS = 1e-6
SCALE = HD ** -0.5
MASKED = 1e32
GELU_C = 0.7978845608028654
SLOPE_STEP = 2.0 ** (-8.0 * R / HEADS)

RING = 4
N_GATE = 0
N_CMP = 1
N_FIRST = [N_CMP + GROUPS]
N_W1 = [N_FIRST[0] + 1]
N_FIRST.append(N_W1[0] + CJ // RING)
N_W1.append(N_FIRST[1] + 1)
N_FIRST += [N_W1[1] + CJ // RING, N_W1[1] + CJ // RING + 1]
N_GRP = N_CMP + GROUPS + 2 * CJ // RING
N_OUT = N_GRP + 4 * GROUPS
N_UP = N_OUT + KT
N_DOWN = N_UP + 2 * FT
N_END = N_DOWN + FT
UNITS = 2 * TB + 1
SCORE_UNITS = [[(0, 1)], [(0, 2)], [(0, 3)], [(0, 0), (1, 0)], [(1, 1)], [(1, 2)], [(1, 3)], 'compressed', None]
SCORED = len(SCORE_UNITS) - 1
U_WIN, U_CMP = 3, 7
STEPS = R * UNITS
AHEAD = 14
BEHIND = 3
W_HID = {-14: (0, 6), -13: (6, 9), -12: (9, 11), -11: (11, 13), -10: (13, 16)}
W_Q = {-9: (0, 2), -8: (2, 4), -7: (4, 6), -6: (6, 8)}
W_V = {-5: (0, 3), -4: (3, 6), -3: (6, 8)}
W_KC, W_GELU, W_GT = -13, -9, -5
TURN = BEHIND + 3
SC_RING, TR_RING, PT_RING = 2, 3, 4
PROJECT = [(6, 4), (12, 4), (19, 5), (26, 5)]
V_POS, V_CB = 0, 2 * CJ
V_A = V_CB + 2 * FT
V_CW = V_A
EARLY = [(9, 0, 0), (13, 0, 1), (17, 0, 2), (21, 0, 3), (24, 2, 3), (26, 3, 3), (28, 0, 4), (30, 2, 5)]
T_OUT = (1, 0, 2, 3)
N_CONST = 11


def slot(n):
    return (n + 3) % RING


def slopes():
    return [2.0 ** (-8.0 * (r + 1) / HEADS) for r in range(R)]


def group_tile(G, i):
    return N_FIRST[i] if first_group(G) else N_GRP + i + RING * G


def first_group(G):
    return isinstance(G, int) and G == 0


def poff(i):
    return P * i * (i + 1) // 2


def scored(w):
    return w // UNITS * SCORED + min(w % UNITS, SCORED)


def unit_cols(w):
    u = w % UNITS
    return T if u == UNITS - 1 else T - P * (u % TB)


def build(nc, x, attn_norm, mlp_norm, final_norm, nsa_w_in, cmp_pos, cmp_w1, cmp_w2, nsa_w_out, mlp_w_up, conv_w, conv_b, mlp_w_down, out):
    ctx = ExitStack()
    w_in, w_out, w_up, w_down = (w[0] for w in (nsa_w_in, nsa_w_out, mlp_w_up, mlp_w_down))
    with ctx:
        place = {"at": (nc.sbuf_base + 31) // 32 * 32}

        def sb(name, shape, dt=F32, at=None):
            size = 4
            for s in shape[1:]:
                size *= s
            off = place["at"] if at is None else at
            if at is None:
                place["at"] = off + (size + 31) // 32 * 32
            assert off + size <= nc.sbuf_usable_end, (name, off + size)
            return nc.alloc_sbuf_tensor_at(name, shape, dt, offset=off), off + (size + 31) // 32 * 32

        def keep(name, shape, dt=F32):
            return sb(name, shape, dt)[0]

        def sem(name):
            return ctx.enter_context(nc.semaphore(name))

        ident = keep("ident", [P, P])
        vec = keep("vec", [P, V_CW + 3 * 2 * FT])
        half_pow = keep("half_pow", [P, TB])
        sumsq = keep("sumsq", [P, 3, TB])
        sumsq_h = keep("sumsq_h", [P, TB, 2])
        meansq = keep("meansq", [P, 3, TB])
        rstd = keep("rstd", [P, 3, TB])
        gates = keep("gates", [P, HEADS, 3, TB])
        valid = keep("valid", [P, 1])
        bias = keep("bias", [P, R, T])
        bias_c = keep("bias_c", [P, R, TB, NC])
        kkc_h = keep("kkc_h", [P, GROUPS, NC], F32R)
        kkc_l = keep("kkc_l", [P, GROUPS, NC], F32R)
        vvc_all = keep("vvc_all", [P, GROUPS, HD])
        xs = keep("xs", [P, TB, D])
        hT_h = keep("hT_h", [P, KT, T], F32R)
        hT_l = keep("hT_l", [P, KT, T], F32R)
        raw = keep("raw", [P, RING, D])
        wh = keep("wh", [P, RING, D], F32R)
        wl = keep("wl", [P, RING, D], F32R)
        base = place["at"]

        def region(specs, at=base):
            made = []
            for name, shape, dt in specs:
                t, at = sb(name, shape, dt, at=at)
                made.append(t)
            return made

        stage, xn, = region([("stage", [P, 2, P], F32), ("xn", [P, TB, D], F32)])
        again, kc2, vc2, glT, gT, blk_h, blk_l, gel, gel2, gTr, w2d, w2v, blk = region([
            ("again", [P, D], F32), ("kc2", [P, GROUPS, TP], F32), ("vc2", [P, GROUPS, TP], F32),
            ("glT", [P, T], F32), ("gT", [P, 2, GROUPS * NC], F32),
            ("blk_h", [P, 2, CJ, GROUPS, NC], F32R), ("blk_l", [P, 2, CJ, GROUPS, NC], F32R),
            ("gel", [P, 2, HID], F32), ("gel2", [P, 2, HID], F32),
            ("gTr", [P, GROUPS, 2, TB, NC], F32), ("w2d", [P, 2, 2, HD], F32), ("w2v", [P, 2, HD], F32),
            ("blk", [P, 2, CJ, GROUPS, NC], F32)], at=base + 3 * P * 4 + TB * D * 4)
        (qq, kk_h, kk_l, vv, vvc, prob, pt_h, pt_l, otmp, osum, oT_h, oT_l, sc_c, pbd, vT, mn, mn_c, sums, rs,
         q_stage, k_stage, v_stage) = region([
            ("qq", [P, R, T], F32R), ("kk_h", [P, 2, T], F32R), ("kk_l", [P, 2, T], F32R),
            ("vv", [P, 2, TB, 2, HD], F32R), ("vvc", [P, 2, HD], F32R), ("prob", [P, 2, 2, poff(TB)], F32),
            ("pt_h", [P, PT_RING, T], F32R), ("pt_l", [P, PT_RING, T], F32R), ("otmp", [P, T], F32), ("osum", [P, 2, T], F32),
            ("oT_h", [P, KT, T], F32R), ("oT_l", [P, KT, T], F32R),
            ("sc_c", [P, 2, TB, NC], F32), ("pbd", [P, 2, TB, TB, NC], F32), ("vT", [P, T], F32),
            ("mn", [P, 2, 2 * TB], F32), ("mn_c", [P, 2, TB], F32), ("sums", [P, 2, 3, TB], F32), ("rs", [P, 2, 3, TB], F32),
            ("q_stage", [P, T], F32), ("k_stage", [P, T], F32), ("v_stage", [P, TB, 2, HD], F32)])
        aT_h, aT_l, conv, th, act, fgain, mgain = region([
            ("aT_h", [P, FT, T], F32R), ("aT_l", [P, FT, T], F32R),
            ("conv", [P, RING, T], F32), ("th", [P, 2, T], F32), ("act", [P, 2, T], F32), ("fgain", [P, D], F32), ("mgain", [P, D], F32)],
            at=base)
        x1n, = region([("x1n", [P, TB, D], F32)], at=base)
        yT, = region([("yT", [P, KT, T], F32)], at=base)

        bank = [ctx.enter_context(nc.psum_tensor(f"bank{n}", [P, 512], F32)) for n in range(8)]
        pj = bank[0:2]
        sc = bank[2:4]
        tr = bank[4:7]
        ob = (bank[7], bank[1])
        def kv_bank(G):
            return pj[1] if first_group(G) else pj[0]
        hid = (bank[7], bank[5])

        x_in = [sem(f"x_in{t}") for t in range(TB)]
        vec_in = sem("vec_in")
        w2_in = sem("w2_in")
        raw_in = [sem(f"raw_in{s}") for s in range(RING)]
        again_in, mgain_in, fgain_in = sem("again_in"), sem("mgain_in"), sem("fgain_in")
        stored = sem("stored")
        const_ready = sem("const_ready")
        stage_clear = sem("stage_clear")
        wh_done, wl_done, tile_done = sem("wh_done"), sem("wl_done"), sem("tile_done")
        sq_done, mean_done, rstd_done, xn_done = sem("sq_done"), sem("mean_done"), sem("rstd_done"), sem("xn_done")
        vecT_ready, vec_done = sem("vecT_ready"), sem("vec_done")
        xT_ready, hT_h_done, hT_done = sem("xT_ready"), sem("hT_h_done"), sem("hT_done")
        pj_evac = sem("pj_evac")
        staged, q_done, k_done, v_done = sem("staged"), sem("q_done"), sem("k_done"), sem("v_done")
        glT_done, gateT_ready, gate_tanh, gates_done = sem("glT_done"), sem("gateT_ready"), sem("gate_tanh"), sem("gates_done")
        c_copied = sem("c_copied")
        blks_done, blkh_done, blk_done = sem("blks_done"), sem("blkh_done"), sem("blk_done")
        gel_step, gel_tanh, gelT_ready, gT_done = sem("gel_step"), sem("gel_tanh"), sem("gelT_ready"), sem("gT_done")
        cmp_ready, kkch_done, cmp_done = sem("cmp_ready"), sem("kkch_done"), sem("cmp_done")
        bias_done, pbd_clear = sem("bias_done"), sem("pbd_clear")
        kvh_done, gel_mid = sem("kvh_done"), sem("gel_mid")
        vvc_done = sem("vvc_done")
        qh_done = sem("qh_done")
        scores_ready, masked, exp_done = sem("scores_ready"), sem("masked"), sem("exp_done")
        c_min, c_shifted, c_exp, c_sum = sem("c_min"), sem("c_shifted"), sem("c_exp"), sem("c_sum")
        recip_done, rs_done, p_scaled, diag_done = sem("recip_done"), sem("rs_done"), sem("p_scaled"), sem("diag_done")
        tr_ready, pth_done, pt_done, av_done = sem("tr_ready"), sem("pth_done"), sem("pt_done"), sem("av_done")
        o_copied, o_summed, oh_done, oT_done = sem("o_copied"), sem("o_summed"), sem("oh_done"), sem("oT_done")
        mask_begun, scale_begun = sem("mask_begun"), sem("scale_begun")
        early_ready, early_done = sem("early_ready"), sem("early_done")
        y_ready, x1_done, half_sum = sem("y_ready"), sem("x1_done"), sem("half_sum")
        conv0, conv1, conv_done = sem("conv0"), sem("conv1"), sem("conv_done")
        g_tanh, silu_done, act_done, ah_done, aT_done = sem("g_tanh"), sem("silu_done"), sem("act_done"), sem("ah_done"), sem("aT_done")
        yT_ready, yT_act, yT_dve, z_ready, x2_done = sem("yT_ready"), sem("yT_act"), sem("yT_dve"), sem("z_ready"), sem("x2_done")
        out_done = sem("out_done")
        C_MASKED = SC_RING
        C_TR = 2 * UNITS
        C_PT = TR_RING
        C_AV = PT_RING
        C_O = 2
        C_CONV = RING
        C_AH = 2

        block = ctx.enter_context(nc.Block())

        def stream_wait(eng, n, m4=None):
            s, k = slot(n), (n + 3) // RING + (slot(n) == 3)
            eng.wait_ge(raw_in[s], 32 * k if m4 is None else 32 * (m4 + k))

        @block.sync
        def _(sp):
            def tile_dma(n, halves, more=None):
                s = slot(n)
                if n >= RING:
                    sp.wait_ge(wl_done, n - RING + 1 if more is None else n - RING + 1 + RING * more)
                for dst, src in halves:
                    sp.dma_start(dst, src).then_inc(raw_in[s], 16)

            def cols(w, s, c0, width=P, at=0):
                src = w.rearrange("(k p) c -> p k c", p=P)
                dst = raw[:, s, :].rearrange("p (k c) -> p k c", c=P)
                return [(dst[:, 4 * h:4 * h + 4, at:at + width], src[:, 4 * h:4 * h + 4, bass.ds(c0, width)]) for h in range(2)]

            def pair(w, s, c0, c1):
                src = w.rearrange("(k p) c -> p k c", p=P)
                dst = raw[:, s, :].rearrange("p (k c) -> p k c", c=P)
                return [(dst[:, :, HD * h:HD * h + HD], src[:, :, bass.ds(c, HD)]) for h, c in enumerate((c0, c1))]

            def rows(w, s, r0):
                return [(raw[:, s, 512 * h:512 * h + 512], w[bass.ds(r0, P), 512 * h:512 * h + 512]) for h in range(2)]

            for t in range(TB):
                sp.dma_start(xs[:, t, :], x[0, t * P:(t + 1) * P, :]).then_inc(x_in[t], 16)
            sp.dma_start(again[:, :], attn_norm.broadcast_to([P, D])).then_inc(again_in, 16)
            tile_dma(N_GATE, cols(w_in, slot(N_GATE), COL_GATE_TILE))
            for g in range(GROUPS):
                tile_dma(N_CMP + g, pair(w_in, slot(N_CMP + g), COL_KC + HD * g, COL_VC + HD * g))

            def group_dma(i, g, n, more=None):
                what = (cols(w_in, slot(n), g * R * HD) if i == 0 else cols(w_in, slot(n), g * R * HD + P) if i == 2
                        else pair(w_in, slot(n), COL_KS + g * HD, COL_KW + g * HD) if i == 1
                        else pair(w_in, slot(n), COL_VS + g * HD, COL_VW + g * HD))
                tile_dma(n, what, more)

            def w1_dma(c):
                for q in range(CJ // RING):
                    n = N_W1[c] + q
                    dst = raw[:, slot(n), :].rearrange("p (j h) -> p j h", h=HID)
                    src = cmp_w1[0, c, 4 * q * P:4 * (q + 1) * P, :].rearrange("(j p) h -> p j h", p=P)
                    tile_dma(n, [(dst[:, 2 * e:2 * e + 2, :], src[:, 2 * e:2 * e + 2, :]) for e in range(2)])

            group_dma(0, 0, N_FIRST[0])
            w1_dma(0)
            group_dma(1, 0, N_FIRST[1])
            w1_dma(1)
            group_dma(2, 0, N_FIRST[2])
            group_dma(3, 0, N_FIRST[3])
            with sp.Fori(0, GROUPS - 1) as g:
                for i in range(4):
                    group_dma(i, g + 1, N_GRP + RING + i, g)
            with sp.Fori(0, KT // RING) as i:
                for j in range(RING):
                    tile_dma(N_OUT + j, rows(w_out, slot(N_OUT + j), i * (RING * P) + j * P), i)
            with sp.Fori(0, FT // 2) as i:
                for j in range(RING):
                    tile_dma(N_UP + j, cols(w_up, slot(N_UP + j), i * (2 * P) + (j // 2) * P + (j % 2) * FF), i)
            for k in range(2):
                tile_dma(N_DOWN + k, rows(w_down, slot(N_DOWN + k), k * P))
            with sp.Fori(0, (FT - 2) // RING) as i:
                for j in range(RING):
                    tile_dma(N_DOWN + 2 + j, rows(w_down, slot(N_DOWN + 2 + j), i * (RING * P) + (2 + j) * P), i)
            for t in range(TB):
                for h in range(2):
                    cols_ = slice(512 * h, 512 * h + 512)
                    sp.wait_ge(out_done, 2 * t + h + 1)
                    sp.dma_start(out[0, t * P:(t + 1) * P, cols_], xs[:, t, cols_]).then_inc(stored, 16)
            sp.wait_ge(stored, 2 * 16 * TB)

        @block.gpsimd
        def _(pool):
            g = nc.gpsimd
            step = [0]

            def then(ins, wait=True):
                step[0] += 1
                ins.then_inc(const_ready, 1)
                if wait:
                    pool.wait_ge(const_ready, step[0])

            g.memset(stage[:, :, :], 0.0).then_inc(stage_clear, 1)
            then(g.memset(half_pow[:, :], -0.5), False)
            then(g.memset(ident[:, :], 0.0))
            then(g.affine_select(out=ident[:, :], in_=ident[:, :], compare_op=ALU.not_equal, fill=1.0, base=0,
                                 pattern=[[-1, P]], channel_multiplier=1))
            then(g.memset(valid[:, :], 1.0))
            then(g.affine_select(out=valid[:, :], in_=valid[:, :], compare_op=ALU.is_ge, fill=0.0, base=-(CMP - 1),
                                 pattern=[[0, 1]], channel_multiplier=1))
            dist, dist_c = bias[:, R - 1, :], bias_c[:, R - 1, :, :]
            then(g.iota(dist, pattern=[[-1, T]], base=T - P, channel_multiplier=1, allow_small_or_imprecise_dtypes=True))
            then(g.affine_select(out=dist, in_=dist, compare_op=ALU.is_ge, fill=MASKED, base=T - P,
                                 pattern=[[-1, T]], channel_multiplier=1))
            then(g.iota(dist_c, pattern=[[P, TB], [-STRIDE, NC]], base=-(CMP - 1), channel_multiplier=1,
                        allow_small_or_imprecise_dtypes=True))
            then(g.affine_select(out=dist_c, in_=dist_c, compare_op=ALU.is_ge, fill=MASKED, base=-(CMP - 1),
                                 pattern=[[P, TB], [-STRIDE, NC]], channel_multiplier=1))

            for z in (kc2, vc2):
                then(g.memset(z[:, :, T - 1:TP], 0.0))
            assert step[0] == N_CONST

            def rstd_of(which, n, t):
                g.tensor_scalar(meansq[:, which, t:t + 1], sumsq[:, which, t:t + 1], 1.0 / D, EPS, ALU.mult, ALU.add).then_inc(mean_done, 1)
                pool.wait_ge(mean_done, TB * which + n + 1)
                g.tensor_tensor(rstd[:, which, t:t + 1], meansq[:, which, t:t + 1], half_pow[:, t:t + 1], ALU.pow).then_inc(rstd_done, 1)

            def low(n, more=None):
                s = slot(n)
                pool.wait_ge(wh_done, n + 1 if more is None else n + 1 + RING * more)
                g.tensor_tensor(wl[:, s, :], raw[:, s, :], wh[:, s, :].bitcast(F32), ALU.subtract).then_inc(wl_done, 1)

            def scale(X, par, b):
                pool.wait_ge(rs_done, 3 * X + 1 + b)
                pool.sem_inc(scale_begun, 1)
                for i in range(TB):
                    p = prob[:, par, b, poff(i):poff(i) + (i + 1) * P]
                    g.tensor_scalar(p, p, rs[:, par, 1 + b, i:i + 1], 1.0, ALU.mult, ALU.mult).then_inc(p_scaled, 1)

            def q_low(G, q):
                for e in range(2):
                    rows_, other = slice(HD * e, HD * e + HD), slice(HD - HD * e, P - HD * e)
                    pool.wait_ge(qh_done, 4 * G + 2 * q + e + 1)
                    g.tensor_tensor(qq[other, 2 * q + e, :], q_stage[rows_, :], qq[rows_, 2 * q + e, :].bitcast(F32), ALU.subtract)\
                        .then_inc(q_done, 1)
                    pool.wait_ge(q_done, 4 * G + 2 * q + e + 1)

            def scale_head(X, par):
                scale(X, par, 0)
                scale(X, par, 1)

            for t in range(TB):
                pool.wait_ge(sq_done, t + 1)
                rstd_of(0, t, t)
            low(N_GATE)
            for n in range(N_CMP, N_GRP + 2 * RING - 1):
                low(n)
                if n == N_FIRST[2] + RING:
                    pool.wait_ge(wl_done, n + 1)
                    q_low(0, 1)
            scale_head(0, 0)
            with pool.Fori(0, GROUPS - 1) as i:
                for r in range(R):
                    scale_head(R * i + r + 1, (r + 1) % 2)
                    if r % 2:
                        pool.wait_ge(p_scaled, 2 * TB * (R * i + r + 2))
                        q_low(i + 1, r // 2)
                    low(N_GRP + 2 * RING - 1 + r, i)
            for r in range(R - 1):
                scale_head(R * (GROUPS - 1) + r + 1, (r + 1) % 2)
                if r == 0:
                    low(N_OUT + RING - 1)
            for n in range(N_OUT + RING, N_UP):
                low(n)
            for n, t in enumerate(T_OUT):
                if n == TB - 1:
                    low(N_UP)
                pool.wait_ge(sq_done, TB + 2 * n + 2)
                g.tensor_tensor(sumsq[:, 1, t:t + 1], sumsq_h[:, t, 0:1], sumsq_h[:, t, 1:2], ALU.add).then_inc(half_sum, 1)
                pool.wait_ge(half_sum, n + 1)
                rstd_of(1, n, t)
            for n in range(N_UP + 1, N_UP + RING):
                low(n)
            with pool.Fori(0, (N_DOWN + FT - 2 - N_UP - RING) // RING) as i:
                for j in range(RING):
                    low(N_UP + RING + j, i)
            for n in range(N_END - 2, N_END):
                low(n)
            for t in range(TB):
                pool.wait_ge(sq_done, 4 * TB + t + 1)
                g.tensor_tensor(sumsq[:, 2, t:t + 1], sumsq_h[:, t, 0:1], sumsq_h[:, t, 1:2], ALU.add).then_inc(half_sum, 1)
                pool.wait_ge(half_sum, TB + t + 1)
                rstd_of(2, t, t)

        @block.scalar
        def _(act_):
            a = nc.scalar

            def high(n, more=None):
                s = slot(n)
                stream_wait(act_, n, more)
                if n >= RING:
                    act_.wait_ge(tile_done, n - RING + 1 if more is None else n - RING + 1 + RING * more)
                a.activation(wh[:, s, :], raw[:, s, :], ACT.Copy).then_inc(wh_done, 1)

            def high_half(n, more, half):
                s, cs = slot(n), slice(D // 2 * half, D // 2 * (half + 1))
                if half == 0:
                    stream_wait(act_, n, more)
                    act_.wait_ge(tile_done, n - RING + 1 + RING * more)
                m = a.activation(wh[:, s, cs], raw[:, s, cs], ACT.Copy)
                if half == 1:
                    m.then_inc(wh_done, 1)

            act_.wait_ge(stage_clear, 1)
            row = 0
            for src, n in ((cmp_pos[0].rearrange("c (j a) d -> (c j) (a d)", a=2), 2 * CJ),
                           (conv_b.rearrange("a (m p) -> (a m) p", p=P), 2 * FT)):
                a.dma_start(stage[row:row + n, 0, :], src).then_inc(vec_in, 16)
                row += n
            taps = conv_w[0].rearrange("i (m p) -> (i m) p", p=P)
            a.dma_start(stage[row:P, 0, :], taps[0:P - row]).then_inc(vec_in, 16)
            a.dma_start(stage[0:V_CW + 3 * 2 * FT - P, 1, :], taps[P - row:3 * 2 * FT]).then_inc(vec_in, 16)
            for e in range(2):
                a.dma_start(w2d[:, :, e, :], cmp_w2[0, 0].rearrange("(h p) d -> p h d", p=P)).then_inc(w2_in, 16)
            a.dma_start(w2v[:, :, :], cmp_w2[0, 1].rearrange("(h p) d -> p h d", p=P)).then_inc(w2_in, 16)

            def square(which, t, junk):
                a.activation(junk, xs[:, t, :], ACT.Square, accum_out=sumsq[:, which, t:t + 1]).then_inc(sq_done, 1)

            def hT_high(which, n, t):
                for h in range(2):
                    act_.wait_ge(xT_ready, 2 * TB * which + 2 * n + h + 1)
                    a.activation(hT_h[:, 4 * h:4 * h + 4, t * P:(t + 1) * P], bank[2 * t + h][:, :].rearrange("p (k c) -> p k c", c=P), ACT.Copy)\
                        .then_inc(hT_h_done, 1)

            for t in range(TB):
                act_.wait_ge(x_in[t], 16)
                square(0, t, xn[:, t, :])
            high(N_GATE)
            for t in range(TB):
                hT_high(0, t, t)
            high(N_CMP)
            high(N_CMP + 1)
            act_.wait_ge(tile_done, N_GATE + 1)
            a.activation(glT[:, :], pj[0][:, :], ACT.Copy).then_inc(glT_done, 1)
            act_.wait_ge(gateT_ready, 1)
            a.activation(gates[:, :, :, :],
                         pj[1][:, :].rearrange("p (i c) -> p i c", c=P)[:, :, GATE_ROW:P].rearrange("p i (h c) -> p h c i", c=3),
                         ACT.Tanh, scale=0.5).then_inc(gate_tanh, 1)
            high(N_CMP + 2)
            high(N_CMP + 3)
            act_.wait_ge(const_ready, N_CONST)
            def blocks_high(half, c):
                for e in range(2):
                    act_.wait_ge(blks_done, 4 * half + 2 * c + e + 1)
                    at = (slice(None), c, slice(CJ // 2 * e, CJ // 2 * (e + 1)), slice(2 * half, 2 * half + 2), slice(None))
                    a.activation(blk_h[at], blk[at], ACT.Copy).then_inc(blkh_done, 1)

            for g in range(GROUPS):
                act_.wait_ge(tile_done, N_CMP + g + 1)
                src = pj[g % 2]
                a.activation(vc2[0:HD, g, 0:T], src[HD:P, :], ACT.Copy).then_inc(c_copied, 1)
                a.activation(vc2[HD:P, g, 0:T - 1], src[HD:P, 1:T], ACT.Copy).then_inc(c_copied, 1)
                high(N_CMP + RING + g)
                if g % 2:
                    blocks_high(g // 2, 0)
                    blocks_high(g // 2, 1)

            def gelu_tanh(c):
                act_.wait_ge(gel_step, 4 * c + 3)
                a.activation(gel2[:, c, :], gel2[:, c, :], ACT.Tanh, scale=GELU_C).then_inc(gel_tanh, 1)

            def exp_unit(G, w):
                r, u = divmod(w, UNITS)
                par = r % 2
                if SCORE_UNITS[u] is None:
                    return
                if u == U_CMP:
                    act_.wait_ge(c_shifted, R * G + r + 1)
                    a.activation(sc_c[:, par, :, :], sc_c[:, par, :, :], ACT.Exp, scale=-1.0).then_inc(c_exp, 1)
                    return
                act_.wait_ge(masked, SCORED * R * G + scored(w) + 1 + C_MASKED)
                for b, i in SCORE_UNITS[u]:
                    p = prob[:, par, b, poff(i):poff(i) + (i + 1) * P]
                    a.activation(p, p, ACT.Exp, scale=-1.0, bias=mn[:, par, TB * b + i:TB * b + i + 1],
                                 accum_out=sums[:, par, 1 + b, i:i + 1]).then_inc(exp_done, 1)

            def pt_high(G, w):
                n = unit_cols(w)
                act_.wait_ge(tr_ready, STEPS * G + w + 1 + C_TR)
                act_.wait_ge(av_done, STEPS * G + w + 1)
                a.activation(pt_h[:, w % PT_RING, 0:n], tr[w % TR_RING][:, 0:n], ACT.Copy).then_inc(pth_done, 1)

            def o_copy(G, r):
                half = (r % 2) * HD
                act_.wait_ge(av_done, STEPS * G + UNITS * (r + 1) + C_AV)
                a.activation(otmp[half:half + HD, :], ob[r % 2][HD:P, :], ACT.Copy).then_inc(o_copied, 1)

            def o_high(G, r):
                half = (r % 2) * HD
                act_.wait_ge(o_summed, R * G + r + 1 + C_O)
                a.activation(oT_h[half:half + HD, bass.ds(2 * G + r // 2, 1), :], osum[half:half + HD, r % 2:r % 2 + 1, :], ACT.Copy)\
                    .then_inc(oh_done, 1)

            def q_copy(G, q):
                act_.wait_ge(tile_done, group_tile(G, 2 * q) + 1)
                if q or not first_group(G):
                    act_.wait_ge(q_done, 4 * G + 2 * q)
                a.activation(q_stage[:, :], pj[0][:, :], ACT.Copy, scale=-SCALE).then_inc(staged, 1)

            def q_high(G, q):
                act_.wait_ge(staged, 5 * G + 1 + 2 * q)
                for e in range(2):
                    rows_ = slice(HD * e, HD * e + HD)
                    a.activation(qq[rows_, 2 * q + e, :], q_stage[rows_, :], ACT.Copy).then_inc(qh_done, 1)

            def k_copy(G):
                act_.wait_ge(tile_done, group_tile(G, 1) + 1)
                if not first_group(G):
                    act_.wait_ge(k_done, 2 * G)
                a.activation(k_stage[:, :], kv_bank(G)[:, :], ACT.Copy).then_inc(staged, 1)

            def k_high(G, b):
                act_.wait_ge(staged, 5 * G + 2)
                for half in (b, 1 - b):
                    a.activation(kk_h[HD * half:HD * half + HD, b, :], k_stage[HD * b:HD * b + HD, :], ACT.Copy).then_inc(kvh_done, 1)

            def vT_copy(G):
                act_.wait_ge(tile_done, group_tile(G, 3) + 1)
                a.activation(vT[:, :], kv_bank(G)[:, :], ACT.Copy).then_inc(staged, 1)

            def v_copy(G):
                act_.wait_ge(gateT_ready, G + 2)
                if not first_group(G):
                    act_.wait_ge(v_done, 2 * G)
                a.activation(v_stage[:, :, :, :], kv_bank(G)[:, :].rearrange("p (t b d) -> p t b d", t=TB, b=2), ACT.Copy).then_inc(staged, 1)

            def v_high(G, b):
                act_.wait_ge(staged, 5 * G + 5)
                a.activation(vv[:, b, :, 0, :], v_stage[:, :, b, :], ACT.Copy).then_inc(kvh_done, 1)

            def steps(G, first, last, project_next):
                for w in range(first, last):
                    r, u = divmod(w, UNITS)
                    if w > BEHIND and u == BEHIND:
                        o_copy(G, r - 1)
                    if 0 <= w and (project_next or w < STEPS):
                        pt_high(G, w)
                    if 0 <= w + AHEAD - 1 and (project_next or w + AHEAD - 1 < STEPS):
                        exp_unit(G, w + AHEAD - 1)
                    if w > BEHIND and u == BEHIND + 1 and r > 0:
                        o_high(G, r - 1)
                    for q in range(CJ // RING):
                        if w - 1 in W_HID and W_HID[w - 1][0] < RING * (q + 1) <= W_HID[w - 1][1]:
                            high(N_W1[1] + q + RING)
                    if w == W_KC + 1:
                        act_.wait_ge(cmp_ready, 1)
                        a.activation(kkc_h[:, :, :].rearrange("p g n -> p (g n)"), bank[6][:, 0:GROUPS * NC], ACT.Copy).then_inc(kkch_done, 1)
                    if w == W_GELU:
                        gelu_tanh(1)
                    if w == -5:
                        q_copy(0, 1)
                        high(N_FIRST[2] + RING)
                        q_high(0, 1)
                    if w == -2:
                        vT_copy(0)
                        high(N_FIRST[3] + RING)
                    if w == -1:
                        v_copy(0)
                        v_high(0, 0)
                    if w == 0:
                        v_high(0, 1)
                    if not project_next:
                        for i, at in enumerate((32, 33, 34, 35)):
                            if w == at:
                                high(N_OUT + RING + i)
                        continue
                    if w == 10:
                        q_copy(G + 1, 0)
                    if w == 11:
                        act_.wait_ge(scores_ready, SCORED * (R * G + 2))
                        q_high(G + 1, 0)
                    if w == 16:
                        k_copy(G + 1)
                    if w == 17:
                        act_.wait_ge(scores_ready, SCORED * (R * G + 3) + U_WIN + 1)
                        k_high(G + 1, 0)
                    if w == 20:
                        act_.wait_ge(scores_ready, SCORED * (R * G + 3) + U_CMP)
                        k_high(G + 1, 1)
                    if w == 24:
                        q_copy(G + 1, 1)
                    if w == 25:
                        act_.wait_ge(scores_ready, SCORED * (R * G + 4))
                        q_high(G + 1, 1)
                    if w == 31:
                        vT_copy(G + 1)
                    if w == 34:
                        v_copy(G + 1)
                    if w == 35:
                        act_.wait_ge(av_done, STEPS * G + STEPS - UNITS + TB + C_AV)
                        v_high(G + 1, 0)
                    if w == 38:
                        act_.wait_ge(av_done, STEPS * G + STEPS - 1 + C_AV)
                        v_high(G + 1, 1)
                    for i, at in enumerate((13, 22, 28, 40)):
                        if w in (at, at + 1):
                            high_half(N_GRP + 2 * RING + i, G, w - at)

            q_copy(0, 0)
            high(N_FIRST[0] + RING)
            q_high(0, 0)
            for n in range(N_W1[0] + RING, N_W1[0] + RING + CJ // RING):
                high(n)
            gelu_tanh(0)
            k_copy(0)
            high(N_FIRST[1] + RING)
            k_high(0, 0)
            k_high(0, 1)
            steps(0, -AHEAD, TURN, True)
            with act_.Fori(0, GROUPS - 1) as G:
                steps(G, TURN, STEPS + TURN, True)
            act_.wait_ge(q_done, 4 * GROUPS)
            act_.wait_ge(k_done, 2 * GROUPS)
            act_.wait_ge(v_done, 2 * GROUPS)
            a.dma_start(mgain[:, :], mlp_norm.broadcast_to([P, D])).then_inc(mgain_in, 16)
            a.dma_start(fgain[:, :], final_norm.rearrange("(a d) -> a d", a=1).broadcast_to([P, D])).then_inc(fgain_in, 16)
            steps(GROUPS - 1, TURN, STEPS + TURN, False)

            def half_square(n, t, h):
                cs = slice(512 * h, 512 * h + 512)
                act_.wait_ge(x1_done, 2 * n + h + 1)
                a.activation(x1n[:, t, cs], xs[:, t, cs], ACT.Square, accum_out=sumsq_h[:, t, h:h + 1]).then_inc(sq_done, 1)

            for n, t in enumerate(T_OUT):
                if n < TB - 1:
                    half_square(n, t, 0)
                else:
                    high(N_UP)
                if n:
                    hT_high(1, n - 1, T_OUT[n - 1])
                if n == TB - 1:
                    high(N_UP + 1)
                    half_square(n, t, 0)
                half_square(n, t, 1)
            high(N_UP + 2)
            hT_high(1, TB - 1, T_OUT[TB - 1])
            high(N_UP + 3)

            with act_.Fori(0, FT // 2) as i:
                for m in range(2):
                    for h in range(2):
                        j = 2 * m + h
                        act_.wait_ge(tile_done, 4 * i + N_UP + j + 1)
                        act_.wait_ge(act_done, 2 * i + m + 1)
                        col = 2 * i + (m + h * FT)
                        a.activation(conv[:, j, :], bank[j][:, :], ACT.Identity,
                                     scale=vec[:, bass.ds(col + (V_CW + 2 * 2 * FT), 1)], bias=vec[:, bass.ds(col + V_CB, 1)])\
                            .then_inc(conv0, 1)
                        high(N_UP + RING + j, i)
                    act_.wait_ge(conv_done, 4 * i + 2 * m + 2 + C_CONV)
                    a.activation(th[:, m, :], conv[:, 2 * m + 1, :], ACT.Tanh, scale=0.5).then_inc(g_tanh, 1)
                    act_.wait_ge(act_done, 2 * i + m + 1 + C_AH)
                    a.activation(aT_h[:, bass.ds(2 * i + m, 1), :], act[:, m:m + 1, :], ACT.Copy).then_inc(ah_done, 1)
            for n in range(N_DOWN + RING, N_DOWN + 2 + RING):
                high(n)
            with act_.Fori(0, (FT - 2 - RING) // RING) as i:
                for j in range(RING):
                    high(N_DOWN + 2 + RING + j, i)
            for n in range(0, KT, 2):
                act_.wait_ge(yT_ready, n + 1)
                a.activation(yT[:, n, :], bank[n][:, :], ACT.Copy).then_inc(yT_act, 1)
            for h in range(2):
                for t in range(TB):
                    act_.wait_ge(x2_done, TB * h + t + 1)
                    cs = slice(512 * h, 512 * h + 512)
                    a.activation(raw[:, t, cs], xs[:, t, cs], ACT.Square, accum_out=sumsq_h[:, t, h:h + 1]).then_inc(sq_done, 1)

        @block.vector
        def _(dve):
            v_ = nc.vector
            dve.sem_inc(masked, C_MASKED)
            dve.sem_inc(pt_done, C_PT)
            dve.sem_inc(o_summed, C_O)
            dve.sem_inc(conv_done, C_CONV)
            dve.sem_inc(act_done, C_AH)

            def normed(which, t, dst, gain):
                dve.wait_ge(rstd_done, TB * which + t + 1)
                v_.scalar_tensor_tensor(dst[:, t, :], xs[:, t, :], rstd[:, which, t:t + 1], gain[:, :], ALU.mult, ALU.mult).then_inc(xn_done, 1)

            def hT_low(which, n, t):
                for h in range(2):
                    dve.wait_ge(hT_h_done, 2 * TB * which + 2 * n + h + 1)
                    dst = (slice(None), slice(4 * h, 4 * h + 4), slice(t * P, (t + 1) * P))
                    v_.tensor_tensor(hT_l[dst], bank[2 * t + h][:, :].rearrange("p (k c) -> p k c", c=P), hT_h[dst].bitcast(F32), ALU.subtract)\
                        .then_inc(hT_done, 1)

            dve.wait_ge(again_in, 16)
            for t in range(TB):
                normed(0, t, xn, again)
                if t:
                    hT_low(0, t - 1, t - 1)
            hT_low(0, TB - 1, TB - 1)
            for n, (c0, c1) in enumerate(((0, P), (P, V_CW + 3 * 2 * FT))):
                dve.wait_ge(vecT_ready, n + 1)
                v_.tensor_copy(vec[:, c0:c1], bank[6 + n][:, 0:c1 - c0]).then_inc(vec_done, 1)
            dve.wait_ge(const_ready, N_CONST)
            for r in range(R):
                s = slopes()[r]
                if r == R - 1:
                    dve.wait_ge(bias_done, 2 * r)
                v_.tensor_scalar(bias[:, r, :], bias[:, R - 1, :], s, None, ALU.mult).then_inc(bias_done, 1)
                v_.tensor_scalar(bias_c[:, r, :, :], bias_c[:, R - 1, :, :], s, None, ALU.mult).then_inc(bias_done, 1)
            dve.wait_ge(gate_tanh, 1)
            v_.tensor_scalar(gates[:, :, :, :], gates[:, :, :, :], 0.5, 0.5, ALU.mult, ALU.add).then_inc(gates_done, 1)
            dve.wait_ge(gates_done, 1)
            v_.tensor_scalar(gates[:, :, 0, 0], gates[:, :, 0, 0], valid[:, 0:1], None, ALU.mult).then_inc(gates_done, 1)

            def at_(half, c, e):
                return slice(None), c, slice(CJ // 2 * e, CJ // 2 * (e + 1)), slice(2 * half, 2 * half + 2), slice(None)

            def blocks(half, c, src):
                gs = slice(2 * half, 2 * half + 2)
                for e in range(2):
                    window = src[:, gs, STRIDE * e:STRIDE * e + T].rearrange("p g (n j two) -> p j g n two", two=2, n=NC)[:, :, :, :, 0]
                    pos = vec[:, V_POS + c * CJ + CJ // 2 * e:V_POS + c * CJ + CJ // 2 * (e + 1)]
                    v_.tensor_tensor(blk[at_(half, c, e)], window,
                                     pos.unsqueeze(2).unsqueeze(3).broadcast_to([P, CJ // 2, 2, NC]), ALU.add).then_inc(blks_done, 1)

            def blocks_low(half, c):
                for e in range(2):
                    n = at_(half, c, e)
                    dve.wait_ge(blkh_done, 4 * half + 2 * c + e + 1)
                    v_.tensor_tensor(blk_l[n], blk[n], blk_h[n].bitcast(F32), ALU.subtract).then_inc(blk_done, 1)

            dve.wait_ge(vec_done, 2)
            for half in range(2):
                for g in (2 * half, 2 * half + 1):
                    dve.wait_ge(tile_done, N_CMP + g + 1)
                    src = pj[g % 2]
                    v_.tensor_copy(kc2[0:HD, g, 0:T], src[0:HD, :])
                    v_.tensor_copy(kc2[HD:P, g, 0:T - 1], src[0:HD, 1:T]).then_inc(pj_evac, 1)
                dve.wait_ge(pj_evac, 2 * half + 2)
                blocks(half, 0, kc2)
                dve.wait_ge(c_copied, 4 * half + 4)
                blocks(half, 1, vc2)
                blocks_low(half, 0)
                blocks_low(half, 1)

            nb = GROUPS * NC

            def gelu(c):
                x_, y_ = gel[:, c, :], gel2[:, c, :]
                dve.wait_ge(tile_done, N_W1[c] + CJ // RING)
                v_.tensor_copy(x_, hid[c][:, 0:HID]).then_inc(gel_step, 1)
                dve.wait_ge(gel_step, 4 * c + 1)
                v_.tensor_tensor(y_, x_, x_, ALU.mult).then_inc(gel_step, 1)
                dve.wait_ge(gel_step, 4 * c + 2)
                v_.tensor_scalar(y_, y_, 0.044715, 1.0, ALU.mult, ALU.add).then_inc(gel_mid, 1)
                dve.wait_ge(gel_mid, 2 * c + 1)
                v_.tensor_tensor(y_, y_, x_, ALU.mult).then_inc(gel_step, 1)

            def gelu_end(c):
                x_, y_ = gel[:, c, :], gel2[:, c, :]
                dve.wait_ge(gel_tanh, c + 1)
                v_.tensor_scalar(y_, y_, 0.5, 0.5, ALU.mult, ALU.add).then_inc(gel_mid, 1)
                dve.wait_ge(gel_mid, 2 * c + 2)
                v_.tensor_tensor(x_, y_, x_, ALU.mult).then_inc(gel_step, 1)

            def mask_unit(G, w):
                r, u = divmod(w, UNITS)
                par, head = r % 2, r % R
                if SCORE_UNITS[u] is None:
                    v_.tensor_scalar(bias[:, head, :], bias[:, head, :], SLOPE_STEP, None, ALU.mult).then_inc(bias_done, 1)
                    v_.tensor_scalar(bias_c[:, head, :, :], bias_c[:, head, :, :], SLOPE_STEP, None, ALU.mult).then_inc(bias_done, 1)
                    return
                src = sc[scored(w) % SC_RING]
                at = SCORED * R * G + scored(w) + 1
                dve.wait_ge(scores_ready, at)
                if u == U_CMP:
                    s = sc_c[:, par, :, :]
                    v_.tensor_tensor(s, src[:, 0:TB * NC].rearrange("p (i n) -> p i n", i=TB), bias_c[:, head, :, :], ALU.add).then_inc(masked, 1)
                    return
                b, i = SCORE_UNITS[u][-1]
                dve.wait_ge(tr_ready, STEPS * G + UNITS * (r - 2) + b * TB + i + 1 + C_TR)
                dve.sem_inc(mask_begun, 1)
                for n_, (b, i) in enumerate(SCORE_UNITS[u]):
                    n = (i + 1) * P
                    m = v_.tensor_tensor_reduce(prob[:, par, b, poff(i):poff(i) + n], src[:, n_ * P:n_ * P + n], bias[:, head, T - n:T], 1.0,
                                                MASKED * 10, ALU.add, ALU.min, mn[:, par, TB * b + i:TB * b + i + 1])
                m.then_inc(masked, 1)

            def c_least(G, r):
                dve.wait_ge(masked, SCORED * (R * G + r) + U_CMP + 1 + C_MASKED)
                v_.tensor_reduce(mn_c[:, r % 2, :], sc_c[:, r % 2, :, :], AX, ALU.min).then_inc(c_min, 1)

            def c_shift(G, r):
                par = r % 2
                dve.wait_ge(c_min, R * G + r + 1)
                v_.tensor_tensor(sc_c[:, par, :, :], sc_c[:, par, :, :], mn_c[:, par, :].unsqueeze(2).broadcast_to([P, TB, NC]), ALU.subtract)\
                    .then_inc(c_shifted, 1)

            def row_sums(G, r):
                dve.wait_ge(c_exp, R * G + r + 1)
                v_.tensor_reduce(sums[:, r % 2, 0, :], sc_c[:, r % 2, :, :], AX, ALU.add).then_inc(c_sum, 1)

            def row_recips(G, r, c):
                X = R * G + r
                if c == 0:
                    dve.wait_ge(c_sum, X + 1)
                else:
                    dve.wait_ge(exp_done, 2 * TB * X + TB * c)
                v_.reciprocal(rs[:, r % 2, c, :], sums[:, r % 2, c, :]).then_inc(recip_done, 1)

            def row_scales(G, r, c):
                par = r % 2
                X, k = R * G + r, {1: 1, 2: 2, 0: 3}[c]
                dve.wait_ge(recip_done, 3 * X + k)
                v_.tensor_tensor(rs[:, par, c:c + 1, :], rs[:, par, c:c + 1, :], gates[:, bass.ds(X, 1), c, :], ALU.mult).then_inc(rs_done, 1)

            def diagonal(G, r):
                par = r % 2
                X = R * G + r
                dve.wait_ge(rs_done, 3 * X + 3)
                dve.wait_ge(tr_ready, STEPS * G + UNITS * (r - 1) + C_TR)
                diag = pbd[:, par, :, :, :].rearrange("p i j n -> p (i j) n")[:, 0:TB * TB:TB + 1, :]
                v_.tensor_tensor(diag, sc_c[:, par, :, :], rs[:, par, 0, :].unsqueeze(2).broadcast_to([P, TB, NC]), ALU.mult).then_inc(diag_done, 1)

            def pt_low(G, w):
                n = unit_cols(w)
                dve.wait_ge(pth_done, STEPS * G + w + 1)
                s = w % PT_RING
                v_.tensor_tensor(pt_l[:, s, 0:n], tr[w % TR_RING][:, 0:n], pt_h[:, s, 0:n].bitcast(F32), ALU.subtract).then_inc(pt_done, 1)

            def o_sum(G, r):
                half = (r % 2) * HD
                dve.wait_ge(o_copied, R * G + r + 1)
                v_.tensor_tensor(osum[half:half + HD, r % 2, :], ob[r % 2][0:HD, :], otmp[half:half + HD, :], ALU.add).then_inc(o_summed, 1)

            def o_low(G, r):
                half = (r % 2) * HD
                dve.wait_ge(oh_done, R * G + r + 1)
                dst = (slice(half, half + HD), bass.ds(2 * G + r // 2, 1), slice(None))
                v_.tensor_tensor(oT_l[dst], osum[half:half + HD, r % 2:r % 2 + 1, :], oT_h[dst].bitcast(F32), ALU.subtract).then_inc(oT_done, 1)

            def k_low(G, b):
                same, other = slice(HD * b, HD * b + HD), slice(HD - HD * b, P - HD * b)
                for n, dst in enumerate((same, other)):
                    dve.wait_ge(kvh_done, 6 * G + 2 * b + 1 + n)
                    m = v_.tensor_tensor(kk_l[dst, b, :], k_stage[same, :], kk_h[same, b, :].bitcast(F32), ALU.subtract)
                m.then_inc(k_done, 1)

            def v_low(G, b):
                dve.wait_ge(kvh_done, 6 * G + 5 + b)
                v_.tensor_tensor(vv[:, b, :, 1, :], v_stage[:, :, b, :], vv[:, b, :, 0, :].bitcast(F32), ALU.subtract).then_inc(v_done, 1)

            def vc_split(G):
                v_.tensor_copy(vvc[:, 0:1, :], vvc_all[:, bass.ds(G, 1), :]).then_inc(vvc_done, 1)
                dve.wait_ge(vvc_done, 2 * G + 1)
                v_.tensor_tensor(vvc[:, 1:2, :], vvc_all[:, bass.ds(G, 1), :], vvc[:, 0:1, :].bitcast(F32), ALU.subtract).then_inc(vvc_done, 1)

            def steps(G, first, last, project_next):
                for w in range(first, last):
                    r, u = divmod(w, UNITS)
                    if u == BEHIND + 1 and r > 0:
                        o_sum(G, r - 1)
                    due = {}
                    for before, what in ((8, 1), (4, 2), (3, 0), (2, None)):
                        X, rest = divmod(w + before, UNITS)
                        if rest == 0 and X >= 0 and (project_next or X < R):
                            due[what] = X
                    cmp_head = (w + AHEAD) // UNITS if (w + AHEAD) % UNITS == U_CMP and (project_next or w + AHEAD < STEPS) else None
                    if 0 in due:
                        row_sums(G, due[0])
                    for c in (1, 2):
                        if c in due:
                            row_recips(G, due[c], c)
                    if project_next or w + AHEAD < STEPS:
                        mask_unit(G, w + AHEAD)
                    if 0 in due:
                        row_recips(G, due[0], 0)
                    if 0 <= w and (project_next or w < STEPS):
                        pt_low(G, w)
                    if cmp_head is not None:
                        c_least(G, cmp_head)
                    for c in (1, 2, 0):
                        if c in due:
                            row_scales(G, due[c], c)
                    if u == BEHIND + 2 and r > 0:
                        o_low(G, r - 1)
                    if None in due:
                        diagonal(G, due[None])
                    if cmp_head is not None:
                        c_shift(G, cmp_head)
                    for x_, (at, b, _) in enumerate(EARLY):
                        if not project_next and w == at + 2:
                            t, cols_ = x_ // 2, slice(512 * (x_ % 2), 512 * (x_ % 2) + 512)
                            if x_ < 2 * TB - 1:
                                dve.wait_ge(early_ready, x_ + 1)
                            else:
                                dve.wait_ge(tile_done, N_OUT + RING)
                            v_.tensor_tensor(xs[:, t, cols_], bank[b][:, :], xs[:, t, cols_], ALU.add).then_inc(early_done, 1)
                    if w == W_KC + 1:
                        dve.wait_ge(kkch_done, 1)
                        v_.tensor_tensor(kkc_l[:, :, :].rearrange("p g n -> p (g n)"), bank[6][:, 0:nb],
                                         kkc_h[:, :, :].rearrange("p g n -> p (g n)").bitcast(F32), ALU.subtract).then_inc(cmp_done, 1)
                    if w == W_GELU:
                        gelu(1)
                    if w == W_GELU + 2:
                        gelu_end(1)
                    if w == W_GT + 1:
                        dve.wait_ge(gelT_ready, 2)
                        for rep in range(TB):
                            v_.tensor_copy(gTr[:, :, :, rep, :], bank[5][:, 0:2 * nb].rearrange("p (a g n) -> p g a n", a=2, g=GROUPS))\
                                .then_inc(gT_done, 1)
                    if w in (-1, 0):
                        v_low(0, w + 1)
                    if w == 1:
                        dve.wait_ge(cmp_ready, 2)
                        v_.tensor_copy(vvc_all[:, :, :], bank[7][:, 0:GROUPS * HD].rearrange("p (g d) -> p g d", g=GROUPS)).then_inc(cmp_done, 1)
                        dve.wait_ge(cmp_done, 2)
                        vc_split(0)
                    if not project_next:
                        continue
                    if w == 18:
                        k_low(G + 1, 0)
                    if w == 21:
                        k_low(G + 1, 1)
                    if w == 36:
                        v_low(G + 1, 0)
                    if w == 39:
                        v_low(G + 1, 1)
                    if w == STEPS + BEHIND:
                        dve.wait_ge(av_done, STEPS * G + STEPS + C_AV)
                        vc_split(G + 1)

            for e in range(2):
                rows_, other = slice(HD * e, HD * e + HD), slice(HD - HD * e, P - HD * e)
                dve.wait_ge(qh_done, e + 1)
                v_.tensor_tensor(qq[other, e, :], q_stage[rows_, :], qq[rows_, e, :].bitcast(F32), ALU.subtract).then_inc(q_done, 1)
            gelu(0)
            gelu_end(0)
            v_.memset(pbd[:, :, :, :, :].rearrange("p a b c n -> p (a b c n)"), 0.0).then_inc(pbd_clear, 1)
            k_low(0, 0)
            k_low(0, 1)
            dve.wait_ge(gelT_ready, 1)
            v_.tensor_copy(gT[:, :, :], bank[4][:, 0:2 * nb].rearrange("p (a n) -> p a n", a=2)).then_inc(gT_done, 1)
            dve.wait_ge(pbd_clear, 1)
            dve.wait_ge(bias_done, 2 * R)
            steps(0, -AHEAD, TURN, True)
            with dve.Fori(0, GROUPS - 1) as G:
                dve.wait_ge(bias_done, 2 * (R * G + R) + 4)
                steps(G, TURN, STEPS + TURN, True)
            steps(GROUPS - 1, TURN, STEPS + TURN, False)

            dve.wait_ge(mgain_in, 16)
            for n, t in enumerate(T_OUT):
                for h in range(2):
                    if 2 * n + h < 2 * TB - 1:
                        dve.wait_ge(y_ready, 2 * n + h + 1)
                    else:
                        dve.wait_ge(tile_done, N_UP)
                    cols_ = slice(512 * h, 512 * h + 512)
                    v_.tensor_tensor(xs[:, t, cols_], bank[2 * t + h][:, :], xs[:, t, cols_], ALU.add).then_inc(x1_done, 1)
                if n:
                    hT_low(1, n - 1, T_OUT[n - 1])
                dve.wait_ge(x1_done, 2 * n + 2)
                dve.wait_ge(rstd_done, TB + n + 1)
                for h in range(2):
                    cols_ = slice(512 * h, 512 * h + 512)
                    v_.scalar_tensor_tensor(x1n[:, t, cols_], xs[:, t, cols_], rstd[:, 1, t:t + 1], mgain[:, cols_], ALU.mult, ALU.mult)\
                        .then_inc(xn_done, 1)
            hT_low(1, TB - 1, T_OUT[TB - 1])

            with dve.Fori(0, FT // 2) as i:
                for m in range(2):
                    for h in range(2):
                        j = 2 * m + h
                        for tap, back in ((1, 1), (0, 2)):
                            dve.wait_ge(conv0 if tap else conv1, 4 * i + j + 1)
                            col = 2 * i + (m + h * FT + V_CW + tap * 2 * FT)
                            v_.scalar_tensor_tensor(conv[:, j, back:T], bank[j][:, 0:T - back], vec[:, bass.ds(col, 1)], conv[:, j, back:T],
                                                    ALU.mult, ALU.add).then_inc(conv1 if tap else conv_done, 1)
                    dve.wait_ge(g_tanh, 2 * i + m + 1)
                    v_.scalar_tensor_tensor(th[:, m, :], th[:, m, :], 1.0, conv[:, 2 * m + 1, :], ALU.add, ALU.mult).then_inc(silu_done, 1)
                    dve.wait_ge(silu_done, 2 * i + m + 1)
                    v_.scalar_tensor_tensor(act[:, m, :], th[:, m, :], 0.5, conv[:, 2 * m, :], ALU.mult, ALU.mult).then_inc(act_done, 1)
                    dve.wait_ge(ah_done, 2 * i + m + 1)
                    v_.tensor_tensor(aT_l[:, bass.ds(2 * i + m, 1), :], act[:, m:m + 1, :], aT_h[:, bass.ds(2 * i + m, 1), :].bitcast(F32),
                                     ALU.subtract).then_inc(aT_done, 1)
            for n in range(1, KT, 2):
                dve.wait_ge(yT_ready, n + 1)
                v_.tensor_copy(yT[:, n, :], bank[n][:, :]).then_inc(yT_dve, 1)

            def result(t, h):
                dve.wait_ge(z_ready, TB * h + t + 1)
                cols_ = slice(512 * h, 512 * h + 512)
                v_.tensor_tensor(xs[:, t, cols_], bank[TB * h + t][:, :], xs[:, t, cols_], ALU.add).then_inc(x2_done, 1)

            for t in range(TB):
                result(t, 0)
            dve.wait_ge(fgain_in, 16)
            for t in range(TB + 2):
                if t < TB:
                    result(t, 1)
                if t >= 2:
                    dve.wait_ge(x2_done, TB + t - 1)
                    dve.wait_ge(rstd_done, 2 * TB + t - 1)
                    for h in range(2):
                        cols_ = slice(512 * h, 512 * h + 512)
                        v_.scalar_tensor_tensor(xs[:, t - 2, cols_], xs[:, t - 2, cols_], rstd[:, 2, t - 2:t - 1], fgain[:, cols_],
                                                ALU.mult, ALU.mult).then_inc(out_done, 1)

        @block.tensor
        def _(pe):
            t_ = nc.tensor
            pe.sem_inc(tr_ready, C_TR)
            pe.sem_inc(av_done, C_AV)

            def xT(which, n, t, src):
                for h in range(2):
                    pe.wait_ge(xn_done, TB + 2 * n + h + 1 if which else n + 1)
                    for k in range(4):
                        m = t_.transpose(bank[2 * t + h][:, k * P:(k + 1) * P], src[:, t, (4 * h + k) * P:(4 * h + k + 1) * P], ident[:, :])
                    m.then_inc(xT_ready, 1)

            def tile_ready(n, more=None):
                pe.wait_ge(wl_done, n + 1 if more is None else n + 1 + RING * more)

            def project(n, dst, more=None, k0=0, k1=KT):
                if k0 == 0:
                    tile_ready(n, more)
                s = slot(n)
                for k in range(k0, k1):
                    c = slice(k * P, (k + 1) * P)
                    t_.matmul(dst[:, :], wh[:, s, c], hT_h[:, k, :], start=(k == 0), stop=False)
                    t_.matmul(dst[:, :], wh[:, s, c], hT_l[:, k, :], start=False, stop=False)
                    m = t_.matmul(dst[:, :], wl[:, s, c], hT_h[:, k, :], start=False, stop=(k == KT - 1))
                if k1 == KT:
                    m.then_inc(tile_done, 1)

            pe.wait_ge(const_ready, 3)
            for t in range(TB):
                xT(0, t, t, xn)
            pe.wait_ge(hT_done, 2 * TB)
            pe.wait_ge(vec_in, 16 * 4)
            for n in range(2):
                t_.transpose(bank[6 + n][:, 0:P], stage[:, n, :], ident[:, :]).then_inc(vecT_ready, 1)
            project(N_GATE, pj[0])
            pe.wait_ge(glT_done, 1)
            for t in range(TB):
                m = t_.transpose(pj[1][:, t * P:(t + 1) * P], glT[:, t * P:(t + 1) * P], ident[:, :])
            m.then_inc(gateT_ready, 1)
            for g in range(GROUPS):
                if g == 1:
                    pe.wait_ge(gate_tanh, 1)
                if g >= 2:
                    pe.wait_ge(pj_evac, g - 1)
                    pe.wait_ge(c_copied, 2 * (g - 1))
                project(N_CMP + g, pj[g % 2])

            def hidden(c, j0=0, j1=CJ):
                for j in range(j0, j1):
                    n, jj = N_W1[c] + j // RING, j % RING
                    if jj == 0:
                        tile_ready(n)
                    pe.wait_ge(blk_done, 4 + 2 * c + 2 * j // CJ + 1)
                    bh, bl = (z[:, c, j, :, :].rearrange("p g n -> p (g n)") for z in (blk_h, blk_l))
                    cs = slice(jj * HID, (jj + 1) * HID)
                    dst = hid[c][:, 0:HID]
                    t_.matmul(dst, bh, wh[:, slot(n), cs], start=(j == 0), stop=False)
                    t_.matmul(dst, bh, wl[:, slot(n), cs], start=False, stop=False)
                    m = t_.matmul(dst, bl, wh[:, slot(n), cs], start=False, stop=(j == CJ - 1))
                    if jj == RING - 1:
                        m.then_inc(tile_done, 1)

            nb = GROUPS * NC

            def gelu_T(c):
                pe.wait_ge(gel_step, 4 * c + 4)
                for h in range(2):
                    m = t_.transpose(bank[4 + c][:, h * nb:h * nb + nb], gel[:, c, h * P:(h + 1) * P], ident[:, :])
                m.then_inc(gelT_ready, 1)

            def second(c):
                pe.wait_ge(gT_done, TB * c + 1)
                pe.wait_ge(w2_in, 48)
                if c == 0:
                    for h in range(2):
                        m = t_.matmul(bank[6][:, 0:nb], w2d[:, h, :, :].rearrange("p e d -> p (e d)"), gT[:, h, :], start=(h == 0), stop=(h == 1))
                else:
                    for g in range(GROUPS):
                        for h in range(2):
                            m = t_.matmul(bank[7][:, g * HD:(g + 1) * HD], gTr[:, g, h, :, :].rearrange("p r n -> p (r n)"), w2v[:, h, :],
                                          start=(h == 0), stop=(h == 1))
                m.then_inc(cmp_ready, 1)

            def score_unit(G, w):
                r, u = divmod(w, UNITS)
                if SCORE_UNITS[u] is None:
                    return
                dst = sc[scored(w) % SC_RING]
                pe.wait_ge(masked, SCORED * R * G + scored(w) + 1)
                if u == U_CMP:
                    kh, kl = (z[:, bass.ds(G + r // R, 1), :].rearrange("p a n -> p (a n)") for z in (kkc_h, kkc_l))
                    for i in range(TB):
                        q = qq[:, r % R, i * P:(i + 1) * P]
                        t_.matmul(dst[:, i * NC:(i + 1) * NC], q, kh, start=True, stop=False)
                        m = t_.matmul(dst[:, i * NC:(i + 1) * NC], q, kl, start=False, stop=True)
                    m.then_inc(scores_ready, 1)
                    return
                b, i = SCORE_UNITS[u][0]
                both = len(SCORE_UNITS[u]) == 2
                n = (i + 1) * P
                q = qq[:, r % R, i * P:(i + 1) * P]
                kh, kl = (z[:, :, 0:n] if both else z[:, b, 0:n] for z in (kk_h, kk_l))
                dst = dst[:, 0:2 * n].rearrange("p (b n) -> p b n", b=2) if both else dst[:, 0:n]
                t_.matmul(dst, q, kh, start=True, stop=False)
                t_.matmul(dst, q, kl, start=False, stop=True).then_inc(scores_ready, 1)

            def transpose_unit(G, w):
                r, u = divmod(w, UNITS)
                b, j = divmod(u, TB)
                X, par, dst = R * G + r, r % 2, tr[w % TR_RING]
                pe.wait_ge(pt_done, STEPS * G + w + 1)
                if u == UNITS - 1:
                    pe.wait_ge(diag_done, X + 1)
                    for i in range(TB):
                        m = t_.transpose(dst[:, i * P:(i + 1) * P], pbd[:, par, i, :, :].rearrange("p j n -> p (j n)"), ident[:, :])
                else:
                    if j == 0:
                        pe.wait_ge(p_scaled, 2 * TB * X + TB * (b + 1))
                    for i in range(j, TB):
                        m = t_.transpose(dst[:, (i - j) * P:(i - j + 1) * P], prob[:, par, b, poff(i) + j * P:poff(i) + (j + 1) * P], ident[:, :])
                m.then_inc(tr_ready, 1)

            def value_unit(G, w):
                r, u = divmod(w, UNITS)
                b, j = divmod(u, TB)
                s, n = w % PT_RING, unit_cols(w)
                if u == 0:
                    pe.wait_ge(o_summed, R * G + r + 1)
                pe.wait_ge(pt_done, STEPS * G + w + 1 + C_PT)
                w_ = (vvc[:, :, :] if u == UNITS - 1 else vv[:, b, j, :, :]).rearrange("p a d -> p (a d)")
                dst = ob[r % 2][:, T - n:T]
                t_.matmul(dst, w_, pt_h[:, s, 0:n], start=(u == 0), stop=False)
                t_.matmul(dst, w_, pt_l[:, s, 0:n], start=False, stop=(u == UNITS - 1)).then_inc(av_done, 1)

            def split(G, queries, keys):
                pe.wait_ge(q_done, 4 * G + 2 * queries)
                pe.wait_ge(k_done, 2 * G + keys)

            def v_transpose(G):
                pe.wait_ge(staged, 5 * G + 4)
                for t in range(TB):
                    m = t_.transpose(kv_bank(G)[:, t * P:(t + 1) * P], vT[:, t * P:(t + 1) * P], ident[:, :])
                m.then_inc(gateT_ready, 1)

            def steps(G, first, last, project_next):
                for w in range(first, last):
                    if w in W_HID:
                        hidden(1, *W_HID[w])
                    if w == W_KC:
                        second(0)
                    if w in W_Q:
                        if w - 1 not in W_Q:
                            pe.wait_ge(staged, 2)
                        project(N_FIRST[2], pj[0], None, *W_Q[w])
                    if w == W_GT:
                        gelu_T(1)
                    if w in W_V:
                        project(N_FIRST[3], pj[1], None, *W_V[w])
                    if w == -1:
                        v_transpose(0)
                    if w == 0:
                        second(1)
                    if project_next or w + AHEAD < STEPS:
                        for at, queries, keys in ((0, 1, 1), (U_WIN, 1, 2), (2 * UNITS, 2, 2)):
                            if w + AHEAD == STEPS + at:
                                split(G + 1, queries, keys)
                            if w + AHEAD == at < TURN + AHEAD:
                                split(G, queries, keys)
                        if w < 0 and w + AHEAD == U_CMP:
                            pe.wait_ge(cmp_done, 1)
                        score_unit(G, w + AHEAD)
                    if w < 0:
                        continue
                    if w == 0:
                        pe.wait_ge(gT_done, 1 + TB)
                    if project_next or w < STEPS:
                        transpose_unit(G, w)
                    if project_next and w >= TURN:
                        for tile in range(4):
                            at, over = PROJECT[tile]
                            k0, k1 = (min(KT, max(0, (w + d - at) * KT // over)) for d in (0, 1))
                            if k1 > k0:
                                if k0 == 0:
                                    pe.wait_ge(staged, 5 * (G + 1) + tile)
                                project(N_GRP + RING + tile, pj[0], G, k0, k1)
                        if w == 33:
                            v_transpose(G + 1)
                    for x_, (at, b, out_) in enumerate(EARLY):
                        if project_next or w not in (at, at + 1):
                            continue
                        t, h = divmod(x_, 2)
                        for k in (2 * (w - at), 2 * (w - at) + 1):
                            if x_ == 0:
                                tile_ready(N_OUT + k)
                            if k == 0 and x_ == 0:
                                pe.wait_ge(oT_done, HEADS // 2)
                                pe.wait_ge(staged, 5 * GROUPS)
                            if k == 0 and out_:
                                pe.wait_ge(early_done, out_)
                            if k == 0 and b:
                                pe.wait_ge(masked, SCORED * HEADS + C_MASKED)
                            s = slot(N_OUT + k)
                            for o, w_ in ((oT_h, wh), (oT_h, wl), (oT_l, wh)):
                                m = t_.matmul(bank[b][:, :], o[:, k, t * P:(t + 1) * P], w_[:, s, 512 * h:512 * h + 512],
                                              start=(k == 0 and o is oT_h and w_ is wh), stop=(k == RING - 1 and o is oT_l))
                            if x_ == 2 * TB - 1:
                                m.then_inc(tile_done, 1)
                            elif k == RING - 1:
                                m.then_inc(early_ready, 1)
                    if w == BEHIND:
                        pe.wait_ge(v_done, 2 * G + 1)
                        pe.wait_ge(cmp_done, 2)
                    if project_next and w == STEPS + BEHIND:
                        pe.wait_ge(v_done, 2 * (G + 1) + 1)
                    if w == TB + BEHIND:
                        pe.wait_ge(v_done, 2 * G + 2)
                        pe.wait_ge(vvc_done, 2 * G + 2)
                    if w >= BEHIND and w - BEHIND < (STEPS + TURN - BEHIND if project_next else STEPS):
                        value_unit(G, w - BEHIND)

            pe.wait_ge(pj_evac, GROUPS - 1)
            pe.wait_ge(c_copied, 2 * (GROUPS - 1))
            project(N_FIRST[0], pj[0])
            hidden(0)
            pe.wait_ge(pj_evac, GROUPS)
            pe.wait_ge(c_copied, 2 * GROUPS)
            project(N_FIRST[1], pj[1])
            gelu_T(0)
            steps(0, -AHEAD, TURN, True)
            with pe.Fori(0, GROUPS - 1) as G:
                steps(G, TURN, STEPS + TURN, True)
            steps(GROUPS - 1, TURN, STEPS + TURN, False)

            def out_product(t, h, ks):
                tc = slice(t * P, (t + 1) * P)
                for k in ks:
                    s = slot(N_OUT + k)
                    for o, w in ((oT_h, wh), (oT_h, wl), (oT_l, wh)):
                        last = k == KT - 1 and o is oT_l
                        m = t_.matmul(bank[2 * t + h][:, :], o[:, k, tc], w[:, s, 512 * h:512 * h + 512],
                                      start=(k == RING and o is oT_h and w is wh), stop=last)
                    if (t, h) == (T_OUT[TB - 1], 1):
                        m.then_inc(tile_done, 1)
                    elif last:
                        m.then_inc(y_ready, 1)

            pe.wait_ge(early_done, 2 * TB)
            early, late = range(RING, RING + 2), range(RING + 2, KT)
            for n, t in enumerate(T_OUT):
                if n == 0:
                    tile_ready(N_OUT + RING + 1)
                    out_product(t, 0, early)
                    out_product(t, 1, early)
                    pe.wait_ge(oT_done, HEADS)
                    tile_ready(N_UP - 1)
                    out_product(t, 0, late)
                    out_product(t, 1, late)
                elif n < TB - 1:
                    out_product(t, 0, range(RING, KT))
                    out_product(t, 1, early)
                    xT(1, n - 1, T_OUT[n - 1], x1n)
                    out_product(t, 1, late)
                else:
                    for k in range(RING, KT):
                        out_product(t, 0, [k])
                        out_product(t, 1, [k])
                        if k == RING + 1:
                            xT(1, n - 1, T_OUT[n - 1], x1n)

            def up_part(j, c0, c1):
                s = slot(N_UP + j)
                for k in range(KT):
                    c = slice(k * P, (k + 1) * P)
                    t_.matmul(bank[j][:, c0:c1], wh[:, s, c], hT_h[:, k, c0:c1], start=(k == 0), stop=False)
                    t_.matmul(bank[j][:, c0:c1], wh[:, s, c], hT_l[:, k, c0:c1], start=False, stop=False)
                    m = t_.matmul(bank[j][:, c0:c1], wl[:, s, c], hT_h[:, k, c0:c1], start=False, stop=(k == KT - 1))
                return m

            pe.wait_ge(hT_done, 4 * TB - 2)
            tile_ready(N_UP)
            up_part(0, 0, T - P)
            xT(1, TB - 1, TB - 1, x1n)
            tile_ready(N_UP + 1)
            up_part(1, 0, T - P)
            pe.wait_ge(hT_done, 4 * TB)
            for j in range(2):
                up_part(j, T - P, T).then_inc(tile_done, 1)
            for j in range(2, RING):
                project(N_UP + j, bank[j])
            with pe.Fori(0, FT // 2 - 1) as i:
                for j in range(RING):
                    pe.wait_ge(conv_done, 4 * i + RING + j + 1)
                    project(N_UP + RING + j, bank[j], i)

            def down(k, n, more=None, last=False):
                pe.wait_ge(aT_done, k + 1)
                tile_ready(n, more)
                s = slot(n)
                first = more is None and n == N_DOWN
                ah, al = aT_h[:, bass.ds(k, 1), :], aT_l[:, bass.ds(k, 1), :]
                ah, al = (z.rearrange("p a t -> p (a t)") for z in (ah, al))
                for c in [*range(RING, KT), *range(RING)] if first else range(KT):
                    if first and c < RING:
                        pe.wait_ge(conv_done, C_CONV + 2 * FT - RING + c + 1)
                    cs = slice(c * P, (c + 1) * P)
                    t_.matmul(bank[c][:, :], wh[:, s, cs], ah, start=first, stop=False, skip_group_check=True)
                    t_.matmul(bank[c][:, :], wh[:, s, cs], al, start=False, stop=False, skip_group_check=True)
                    m = t_.matmul(bank[c][:, :], wl[:, s, cs], ah, start=False, stop=last, skip_group_check=True)
                    if last:
                        m.then_inc(yT_ready, 1)
                if not last:
                    m.then_inc(tile_done, 1)

            for k in range(2):
                down(k, N_DOWN + k)
            with pe.Fori(0, (FT - 2 - RING) // RING) as i:
                for j in range(RING):
                    down(i * RING + (2 + j), N_DOWN + 2 + j, i)
            for k in range(FT - RING, FT):
                down(k, N_DOWN + k, None, k == FT - 1)
            for h in range(2):
                pe.wait_ge(yT_act, 2 * (h + 1))
                pe.wait_ge(yT_dve, 2 * (h + 1))
                for t in range(TB):
                    for c in range(4):
                        m = t_.transpose(bank[TB * h + t][:, c * P:(c + 1) * P], yT[:, 4 * h + c, t * P:(t + 1) * P], ident[:, :])
                    m.then_inc(z_ready, 1)


_INS = ['x', 'attn_norm', 'mlp_norm', 'final_norm', 'nsa_w_in', 'nsa_cmp_pos', 'nsa_cmp_w1', 'nsa_cmp_w2', 'nsa_w_out',
        'mlp_w_up', 'mlp_conv_w', 'mlp_conv_b', 'mlp_w_down']


def kernel(**inputs):
    import numpy as _np
    import concourse.bacc as _bacc
    from concourse import mybir as _mybir
    from concourse.bass_utils import run_bass_kernel_spmd as _run

    nc = _bacc.Bacc("TRN2", target_bir_lowering=False, num_devices=1, dynamic_dma_scratch_size=1024)
    arrays, args = {}, []
    for name in _INS:
        a = _np.ascontiguousarray(inputs[name])
        arrays[f"in_{name}"] = a
        args.append(nc.dram_tensor(f"in_{name}", a.shape, _mybir.dt.from_np(a.dtype), kind="ExternalInput").ap())
    args.append(nc.dram_tensor("out_x", (1, T, D), F32, kind="ExternalOutput").ap())
    build(nc, *args)
    r = _run(nc, [arrays], core_ids=[0])
    return r.results[0]["out_x"]
```
